# Optimizing a Trainium2 kernel written in Bass

```python
import math
import jax
import jax.numpy as jnp
from jax import lax
import numpy as np

D_MODEL = 2048
BATCH = 1
SEQ = 256
DEPTH = 2

HEAD_DIM = 128
HEADS_PER_MIXER = D_MODEL // HEAD_DIM // 4
D_MIX = 4 * HEADS_PER_MIXER * HEAD_DIM
Q_BLOCK = 128
GRID_W = 64
NORM_EPS = 1e-6
ROPE_THETA = 10000.0

A_HEADS = HEADS_PER_MIXER
A_HALF = HEAD_DIM // 2
B_HEADS = HEADS_PER_MIXER
B_Q_RANK = 512
B_KV_RANK = 256
B_NOPE = 128
B_ROPE = 64
B_V = HEAD_DIM
C_HEADS = HEADS_PER_MIXER
C_KV_HEADS = C_HEADS // 2
D_HEADS = HEADS_PER_MIXER
D_PATTERNS = ((128, 1), (512, 4), (2048, 16))
D_PAD = max(w // 2 for w, _ in D_PATTERNS)

REL_BUCKETS = 32
REL_MAX_DIST = 1024
REL_HEADS = A_HEADS + D_HEADS

FFN_HIDDEN = -(-(8 * D_MODEL) // (3 * 256)) * 256

A_W = A_HEADS * HEAD_DIM
C_QW = C_HEADS * HEAD_DIM
C_KVW = C_KV_HEADS * HEAD_DIM
D_W = D_HEADS * HEAD_DIM
IN_SIZES = (A_W, A_W, A_W, B_Q_RANK, B_KV_RANK, B_ROPE, C_QW, C_KVW, C_KVW, D_W, D_W, D_W)
IN_COLS = sum(IN_SIZES)
SPLIT_POINTS = tuple(sum(IN_SIZES[:i + 1]) for i in range(len(IN_SIZES) - 1))

kernel_name = 'hybrid_parallel_head_encoder'

def _rmsnorm(x, g):
    xf = x.astype(jnp.float32)
    y = xf * lax.rsqrt(jnp.mean(xf * xf, axis=-1, keepdims=True) + NORM_EPS)
    return (y * g.astype(jnp.float32)).astype(x.dtype)

def _rope_cos_sin(pos, dim):
    inv = ROPE_THETA ** (-jnp.arange(0, dim, 2, dtype=jnp.float32) / dim)
    ang = pos.astype(jnp.float32)[:, None] * inv[None, :]
    return jnp.cos(ang), jnp.sin(ang)

def _apply_rope(x, cos, sin):
    half = x.shape[-1] // 2
    x1 = x[..., :half].astype(jnp.float32)
    x2 = x[..., half:].astype(jnp.float32)
    c = cos[None, :, None, :]
    s = sin[None, :, None, :]
    return jnp.concatenate([x1 * c - x2 * s, x2 * c + x1 * s], axis=-1).astype(x.dtype)

def _axial_rope(x, cos_r, sin_r, cos_c, sin_c):
    half = x.shape[-1] // 2
    return jnp.concatenate([_apply_rope(x[..., :half], cos_r, sin_r),
                            _apply_rope(x[..., half:], cos_c, sin_c)], axis=-1)

def _t5_bucket(rel):
    half = REL_BUCKETS // 2
    max_exact = half // 2
    ret = jnp.where(rel > 0, half, 0)
    n = jnp.abs(rel)
    nf = jnp.maximum(n, max_exact).astype(jnp.float32)
    large = max_exact + (jnp.log(nf / max_exact) / math.log(REL_MAX_DIST / max_exact)
                         * (half - max_exact)).astype(jnp.int32)
    large = jnp.minimum(large, half - 1)
    return ret + jnp.where(n < max_exact, n, large)

def _blocked_attention(q, k, v):
    b, s, hq, dq = q.shape
    hk = k.shape[2]
    g = hq // hk
    nb = s // Q_BLOCK
    scale = dq ** -0.5
    qblocks = jnp.swapaxes(q.reshape(b, nb, Q_BLOCK, hk, g, dq), 0, 1)

    def block(qb):
        logits = jnp.einsum('bqhgd,bkhd->bhgqk', qb, k).astype(jnp.float32) * scale
        p = jax.nn.softmax(logits, axis=-1)
        return jnp.einsum('bhgqk,bkhd->bqhgd', p.astype(v.dtype), v)

    o = lax.map(block, qblocks)
    return jnp.swapaxes(o, 0, 1).reshape(b, s, hq, v.shape[-1])

def _diff_attention(q, k, v, lam, bias_table):
    b, s = q.shape[0], q.shape[1]
    nb = s // Q_BLOCK
    scale = A_HALF ** -0.5
    kpos = jnp.arange(s, dtype=jnp.int32)
    qblocks = jnp.swapaxes(q.reshape(b, nb, Q_BLOCK, A_HEADS, 2, A_HALF), 0, 1)
    starts = jnp.arange(nb, dtype=jnp.int32) * Q_BLOCK

    def block(args):
        qb, start = args
        qpos = start + jnp.arange(Q_BLOCK, dtype=jnp.int32)
        bias = bias_table[_t5_bucket(kpos[None, :] - qpos[:, None])].astype(jnp.float32)
        logits = jnp.einsum('bqhmd,bkhmd->bmhqk', qb, k).astype(jnp.float32) * scale
        logits = logits + jnp.transpose(bias, (2, 0, 1))[None, None]
        p = jax.nn.softmax(logits, axis=-1)
        w = p[:, 0] - lam * p[:, 1]
        return jnp.einsum('bhqk,bkhd->bqhd', w.astype(v.dtype), v)

    o = lax.map(block, (qblocks, starts))
    return jnp.swapaxes(o, 0, 1).reshape(b, s, A_HEADS, HEAD_DIM)

def _dilated_offsets():
    rows = []
    for w, r in D_PATTERNS:
        n = (w // 2) // r
        rows.append(np.arange(-n, n + 1, dtype=np.int32) * r)
    return jnp.asarray(np.stack(rows))

def _dilated_attention(q, k, v, bias_table):
    b, s, h, d = q.shape
    nb = s // Q_BLOCK
    scale = d ** -0.5
    offs = _dilated_offsets()
    bias = jnp.transpose(bias_table[_t5_bucket(offs)], (0, 2, 1)).astype(jnp.float32)
    pad = ((0, 0), (D_PAD, D_PAD), (0, 0), (0, 0))
    kp = jnp.pad(k, pad)
    vp = jnp.pad(v, pad)
    qblocks = jnp.swapaxes(q.reshape(b, nb, Q_BLOCK, h, d), 0, 1)
    starts = jnp.arange(nb, dtype=jnp.int32) * Q_BLOCK

    def block(args):
        qb, start = args
        qpos = start + jnp.arange(Q_BLOCK, dtype=jnp.int32)
        kpos = qpos[:, None, None] + offs[None]
        valid = (kpos >= 0) & (kpos < s)
        kg = kp[:, kpos + D_PAD]
        vg = vp[:, kpos + D_PAD]
        logits = jnp.einsum('bqhd,bqpjhd->bqphj', qb, kg).astype(jnp.float32) * scale + bias[None, None]
        logits = jnp.where(valid[None, :, :, None, :], logits, -jnp.inf)
        lse = jax.nn.logsumexp(logits, axis=-1)
        p = jnp.exp(logits - lse[..., None])
        o = jnp.einsum('bqphj,bqpjhd->bqphd', p.astype(v.dtype), vg)
        alpha = jax.nn.softmax(lse, axis=2)
        return jnp.einsum('bqph,bqphd->bqhd', alpha.astype(v.dtype), o)

    o = lax.map(block, (qblocks, starts))
    return jnp.swapaxes(o, 0, 1).reshape(b, s, h, d)

def setup_inputs(seed: int = 0) -> dict:
    key = jax.random.key(seed)
    ks = jax.random.split(key, 18)
    f32 = jnp.float32

    def nrm(k, shape, scale):
        return jax.random.normal(k, shape, f32) * scale

    def gain(k, shape):
        return 1.0 + 0.02 * jax.random.normal(k, shape, f32)

    return {
        'x': nrm(ks[0], (BATCH, SEQ, D_MODEL), 1.0),
        'rel_bias': nrm(ks[1], (REL_BUCKETS, REL_HEADS), 0.5),
        'norm_mix_pre': gain(ks[2], (DEPTH, D_MODEL)),
        'norm_mix_post': gain(ks[3], (DEPTH, D_MODEL)),
        'norm_ffn_pre': gain(ks[4], (DEPTH, D_MODEL)),
        'norm_ffn_post': gain(ks[5], (DEPTH, D_MODEL)),
        'w_in': nrm(ks[6], (DEPTH, D_MODEL, IN_COLS), D_MODEL ** -0.5),
        'diff_lambda': nrm(ks[7], (DEPTH, 4, A_HALF), 0.1),
        'diff_subln': gain(ks[8], (DEPTH, HEAD_DIM)),
        'mla_q_norm': gain(ks[9], (DEPTH, B_Q_RANK)),
        'mla_kv_norm': gain(ks[10], (DEPTH, B_KV_RANK)),
        'mla_w_uq': nrm(ks[11], (DEPTH, B_Q_RANK, B_HEADS * (B_NOPE + B_ROPE)), B_Q_RANK ** -0.5),
        'mla_w_ukv': nrm(ks[12], (DEPTH, B_KV_RANK, B_HEADS * (B_NOPE + B_V)), B_KV_RANK ** -0.5),
        'gqa_q_norm': gain(ks[13], (DEPTH, HEAD_DIM)),
        'gqa_k_norm': gain(ks[14], (DEPTH, HEAD_DIM)),
        'w_out': nrm(ks[15], (DEPTH, D_MIX, D_MODEL), D_MIX ** -0.5),
        'w_gate_up': nrm(ks[16], (DEPTH, D_MODEL, 2 * FFN_HIDDEN), D_MODEL ** -0.5),
        'w_down': nrm(ks[17], (DEPTH, FFN_HIDDEN, D_MODEL), FFN_HIDDEN ** -0.5),
    }

def reference(x, rel_bias, norm_mix_pre, norm_mix_post, norm_ffn_pre, norm_ffn_post, w_in,
              diff_lambda, diff_subln, mla_q_norm, mla_kv_norm, mla_w_uq, mla_w_ukv,
              gqa_q_norm, gqa_k_norm, w_out, w_gate_up, w_down):
    b, s, _ = x.shape
    rows = s // GRID_W
    pos = jnp.arange(s, dtype=jnp.int32)
    row_idx = jnp.repeat(jnp.arange(rows, dtype=jnp.int32), GRID_W)
    col_idx = pos % GRID_W
    cos_1d, sin_1d = _rope_cos_sin(pos, B_ROPE)
    cos_r, sin_r = _rope_cos_sin(row_idx, HEAD_DIM // 2)
    cos_c, sin_c = _rope_cos_sin(col_idx, HEAD_DIM // 2)
    bias_a = rel_bias[:, :A_HEADS]
    bias_d = rel_bias[:, A_HEADS:]

    for l in range(DEPTH):
        h = _rmsnorm(x, norm_mix_pre[l])
        (a_q, a_k, a_v, b_cq, b_ckv, b_kpe, c_q, c_k, c_v, d_q, d_k, d_v) = jnp.split(
            h @ w_in[l], SPLIT_POINTS, axis=-1)

        lam_init = 0.8 - 0.6 * math.exp(-0.3 * l)
        lv = diff_lambda[l].astype(jnp.float32)
        lam = jnp.exp(jnp.sum(lv[0] * lv[1])) - jnp.exp(jnp.sum(lv[2] * lv[3])) + lam_init
        o_a = _diff_attention(a_q.reshape(b, s, A_HEADS, 2, A_HALF),
                              a_k.reshape(b, s, A_HEADS, 2, A_HALF),
                              a_v.reshape(b, s, A_HEADS, HEAD_DIM), lam, bias_a)
        o_a = _rmsnorm(o_a, diff_subln[l]) * (1.0 - lam_init)

        q_b = (_rmsnorm(b_cq, mla_q_norm[l]) @ mla_w_uq[l]).reshape(b, s, B_HEADS, B_NOPE + B_ROPE)
        kv_b = (_rmsnorm(b_ckv, mla_kv_norm[l]) @ mla_w_ukv[l]).reshape(b, s, B_HEADS, B_NOPE + B_V)
        q_b = jnp.concatenate([q_b[..., :B_NOPE], _apply_rope(q_b[..., B_NOPE:], cos_1d, sin_1d)], axis=-1)
        k_pe = jnp.broadcast_to(_apply_rope(b_kpe[:, :, None, :], cos_1d, sin_1d), (b, s, B_HEADS, B_ROPE))
        k_b = jnp.concatenate([kv_b[..., :B_NOPE], k_pe], axis=-1)
        o_b = _blocked_attention(q_b, k_b, kv_b[..., B_NOPE:])

        q_c = _axial_rope(_rmsnorm(c_q.reshape(b, s, C_HEADS, HEAD_DIM), gqa_q_norm[l]), cos_r, sin_r, cos_c, sin_c)
        k_c = _axial_rope(_rmsnorm(c_k.reshape(b, s, C_KV_HEADS, HEAD_DIM), gqa_k_norm[l]), cos_r, sin_r, cos_c, sin_c)
        o_c = _blocked_attention(q_c, k_c, c_v.reshape(b, s, C_KV_HEADS, HEAD_DIM))

        o_d = _dilated_attention(d_q.reshape(b, s, D_HEADS, HEAD_DIM),
                                 d_k.reshape(b, s, D_HEADS, HEAD_DIM),
                                 d_v.reshape(b, s, D_HEADS, HEAD_DIM), bias_d)

        mix = jnp.concatenate([o_a, o_b, o_c, o_d], axis=2).reshape(b, s, D_MIX)
        x = x + _rmsnorm(mix @ w_out[l], norm_mix_post[l])

        h = _rmsnorm(x, norm_ffn_pre[l])
        gate, up = jnp.split(h @ w_gate_up[l], 2, axis=-1)
        x = x + _rmsnorm((jax.nn.silu(gate) * up) @ w_down[l], norm_ffn_post[l])
    return x


_drawn_inputs = setup_inputs


def setup_inputs(seed=0):
    import zlib

    import numpy as np

    out = dict(_drawn_inputs(seed))
    spreads = {}
    factors = {'norm_ffn_post': 3.565,
     'diff_subln': 8.936,
     'mla_q_norm': 8.0,
     'mla_kv_norm': 8.0,
     'gqa_q_norm': 8.0,
     'gqa_k_norm': 8.0}
    for name, (base, spread) in spreads.items():
        noise = np.random.default_rng([zlib.crc32(name.encode()), seed]).standard_normal(out[name].shape)
        drawn = base * np.exp(spread * noise) if base else spread * noise
        out[name] = jnp.asarray(drawn.astype(out[name].dtype))
    for name, factor in factors.items():
        out[name] = (out[name] * factor).astype(out[name].dtype)
    return out
```

```python
from contextlib import ExitStack

import numpy as np
import concourse.bass as bass
from concourse import mybir
from concourse.alu_op_type import AluOpType as ALU

F32 = mybir.dt.float32
F32R = mybir.dt.float32r
ACT = mybir.ActivationFunctionType
AX_X = mybir.AxisListType.X

P = 128
LAYERS, D, SEQ = 2, 2048, 256
TT = SEQ // P
KT = D // P
HID = 5632
EPS = 1e-6
SLAB = 2048
CH = 512

A_Q, A_K, A_V, B_CQ, B_CKV, B_KPE = 0, 512, 1024, 1536, 2048, 2304
C_Q, C_K, C_V, D_Q, D_K, D_V = 2560, 3072, 3328, 3584, 4096, 4608
PAD_AT, PAD = 2368, 192
IN_COLS = 4928
Q_RANK, KV_RANK, NOPE, ROPE = 512, 256, 128, 64
C_HEADS, C_KV = 4, 2

IN_ORDER = ((B_CQ, 512), (B_CKV, 320), (C_Q, 512), (C_K, 512),
            (A_Q, 512), (A_K, 512), (A_V, 512), (D_Q, 512), (D_K, 512), (D_V, 512))
MLA_SIZE = (2048, 1024, 1024, 1024)
GU_CHUNKS, DN_SLABS = 22, 44

FRONT = [("in", c, j, IN_ORDER[c][1]) for c in range(4) for j in range(4)]
FRONT += [("mla", j, 0, (512, 256, 512, 512)[j]) for j in range(4)]
FRONT += [("in", c, j, 512) for c in range(4, 10) for j in range(4)]
S_OUT = len(FRONT)
FRONT += [("out", c, j, CH) for c in range(2) for j in range(3)] + [("out", 0, 3, CH), ("out", 1, 3, CH)]
FRONT += [("out", c, j, CH) for c in range(2, 4) for j in range(4)]
S_MLA = 16
S_GU = len(FRONT)
S_DN = S_GU + 4 * GU_CHUNKS
SLABS = S_DN + DN_SLABS
SIZE = [MLA_SIZE[f[1]] if f[0] == "mla" else SLAB for f in FRONT]

ENDS = [("in", c) for c in range(4)] + [("mla", j) for j in range(4)] + [("in", c) for c in range(4, 10)]
ENDS += [("out", c) for c in range(4)]
C_GU = len(ENDS)
C_DN = C_GU + GU_CHUNKS
CHUNKS = C_DN + 4
ORDER = {e: n for n, e in enumerate(ENDS)}


def last_slab(chunk):
    return max(s for s, f in enumerate(FRONT) if f[:2] == chunk)


ENDED = {last_slab(e): e for e in ENDS}

G_MIX, G_FFN, G_CQ, G_CKV, G_SUB, LAM0, ONE_LAM0 = 0, 16, 32, 36, 38, 39, 40
N_COLS = 41
G_CQN, G_CKN = 41, 41 + P
N_SMALL = 41 + 2 * P

UNITS = [(g, h) for g in "BCAD" for h in range(4)]
NU = len(UNITS)
FIRST = {"B": 42, "C": 54, "A": 66, "D": 83}
START = {FIRST[g] + 3 * h: u for u, (g, h) in enumerate(UNITS)}
SCORE, EXP, TURN, OUT = 1, 2, 4, 5
LATENT_AT = 20
SQ_C_AT = 46
A_SQUARE, A_NORM, A_TURN = 81, 85, (88, 90)
MIX_AT = {"B": 0, "C": 4, "A": 8, "D": 12}


def unit(half, step):
    return START.get(half - step)




def build(nc, x_d, w_in, w_mla, w_out, w_gu, w_dn, small_d, gqa_d, post_mix, post_ffn, lam_d, rel_d,
          onehot_d, lncount_d, ident_d, flip_d, rope_d, axial_d, out_d):
    ctx = ExitStack()
    with ctx:
        def sb(name, shape, dt=F32):
            return ctx.enter_context(nc.sbuf_tensor(name, shape, dt))

        def sem(name):
            return ctx.enter_context(nc.semaphore(name))

        ps = ctx.enter_context(nc.psum_tensor("ps", [P, 8, CH], F32))
        rel_rows = nc.dram_tensor("rel_rows", (8, 512), F32, kind="Internal").ap()

        x = sb("x", [P, TT, D])
        y = sb("y", [P, TT, D])
        h_hi = sb("h_hi", [P, KT, SEQ], F32R)
        h_lo = sb("h_lo", [P, KT, SEQ], F32R)
        big = sb("big", [P, 44 * SEQ])
        qkv = big[:, 0:TT * 5120].rearrange("p (t n) -> p t n", t=TT)
        hid = big[:, :].rearrange("p (k n) -> p k n", k=44)
        raw = sb("raw", [P, 2, SLAB])
        w_hi = sb("w_hi", [P, 2, SLAB], F32R)
        w_lo = sb("w_lo", [P, 2, SLAB], F32R)
        bias = sb("bias", [P, 8, SEQ + P])
        c_hi = sb("c_hi", [P, 6, SEQ], F32R)
        c_lo = sb("c_lo", [P, 6, SEQ], F32R)
        work = sb("work", [P, 3072])
        qkT = work[:, 0:512]
        PT = work[:, 512:1024]
        prob = work[:, 1024:3072].rearrange("p (b m n) -> p b m n", b=2, m=2)
        gpost = work[:, 1024:3072]
        y_flat = y[:].rearrange("p t n -> p (t n)")
        sg = y_flat[:, 0:1024].rearrange("p (b t n) -> p b t n", b=2, t=TT)
        act_tile = y_flat[:, 1024:2048].rearrange("p (b t n) -> p b t n", b=2, t=TT)
        qrT = sb("qrT", [64, SEQ])
        kpeT = sb("kpeT", [64, SEQ])
        tmp = sb("tmp", [P, 1536])
        ident = sb("ident", [P, P])
        rope = sb("rope", [P, TT, 2, 32])
        axial = sb("axial", [P, 2, TT, 2, 32])
        small_all = sb("small_all", [P, LAYERS, N_SMALL])
        small = sb("small", [P, N_SMALL])
        lam_in = work[:, 0:LAYERS * 256].rearrange("p (l f d) -> p l f d", l=LAYERS, f=4)
        lam_prod = sb("lam_prod", [P, LAYERS * 2, 64])
        lam_e = sb("lam_e", [P, LAYERS, 2])
        lam_d1 = sb("lam_d1", [P, LAYERS])
        lam_all = sb("lam_all", [P, LAYERS])
        lam = sb("lam", [P, 1])
        gsub = sb("gsub", [P, 1])
        mhalf = sb("mhalf", [P, 12])
        eps_row = sb("eps_row", [P, 12])
        inv_head = sb("inv_head", [P, 12])
        inv_rank = sb("inv_rank", [P, 4])
        xss = sb("xss", [P, TT])
        xvar = sb("xvar", [P, TT])
        rs = sb("rs", [P, TT])
        yss = sb("yss", [P, TT, 4])
        ysum = sb("ysum", [P, TT])
        yvar = sb("yvar", [P, TT])
        rsy = sb("rsy", [P, TT])
        bss = sb("bss", [P, 4])
        bmean = sb("bmean", [P, 4])
        bvar = sb("bvar", [P, 4])
        brs = sb("brs", [P, 4])
        css = sb("css", [P, 12])
        cmean = sb("cmean", [P, 12])
        cvar = sb("cvar", [P, 12])
        crs = sb("crs", [P, 12])
        ass = sb("ass", [P, 8])
        amean = sb("amean", [P, 8])
        avar = sb("avar", [P, 8])
        ars = sb("ars", [P, 8])
        mx = sb("mx", [P, 2, 4])
        nmax = sb("nmax", [P, 2, 4])
        esum = sb("esum", [P, 2, 4])
        rsum = sb("rsum", [P, 2, 4])
        rlam = sb("rlam", [P, 2, 2])
        bias_rev = y_flat[:, 0:8 * (SEQ + P)].rearrange("p (h n) -> p h n", h=8)
        flip = work[:, 512:512 + P]
        oh_s = tmp[0:32, 0:512]
        rel_s = tmp[0:32, 512:520]
        lnc_s = tmp[0:8, 1024:1536]
        relrow_s = tmp[0:8, 0:512]
        qb = y[:, :, 0:768]
        kvb = y[:, :, 768:1792]

        loaded = [sem("loaded0"), sem("loaded1")]
        hi_done = sem("hi_done")
        lo_done = sem("lo_done")
        used = sem("used")
        acc_free = sem("acc_free")
        x_load = sem("x_load")
        x_ready = sem("x_ready")
        c_load = sem("c_load")
        r_load = sem("r_load")
        rel_mm, rel_sum, rel_out, rel_in = sem("rel_mm"), sem("rel_sum"), sem("rel_out"), sem("rel_in")
        flip_mm, flip_out = sem("flip_mm"), sem("flip_out")
        set_up = sem("set_up")
        lam_v, lam_a = sem("lam_v"), sem("lam_a")
        params = sem("params")
        hx_tr, hx_hi, hx_lo = sem("hx_tr"), sem("hx_hi"), sem("hx_lo")
        xsq, rs_ok = sem("xsq"), sem("rs_ok")
        post_load = sem("post_load")
        y_sq, y_sum, rsy_ok = sem("y_sq"), sem("y_sum"), sem("rsy_ok")
        sq_b, sq_c, ss_b, ss_c = sem("sq_b"), sem("sq_c"), sem("ss_b"), sem("ss_c")
        brs_ok, kpe_ok, c_ok, bq_ok = sem("brs_ok"), sem("kpe_ok"), sem("c_ok"), sem("bq_ok")
        ct_tr, ct_hi, ct_lo = sem("ct_tr"), sem("ct_hi"), sem("ct_lo")
        t_done, t_out = sem("t_done"), sem("t_out")
        s_done, m_ok, e_done, p_ok = sem("s_done"), sem("m_ok"), sem("e_done"), sem("p_ok")
        pt_done, pt_out = sem("pt_done"), sem("pt_out")
        o_done, o_hi, o_out = sem("o_done"), sem("o_hi"), sem("o_out")
        ao_ss, ao_rs, ao_n, ao_tr, ao_hi, ao_lo = (sem(n) for n in ("ao_ss", "ao_rs", "ao_n", "ao_tr", "ao_hi", "ao_lo"))
        sw_g = sem("sw_g")
        ht_tr = sem("ht_tr")
        ht_out = sem("ht_out")
        mix_hi, mix_lo = sem("mix_hi"), sem("mix_lo")
        hid_hi_ok, hid_lo_ok = sem("hid_hi_ok"), sem("hid_lo_ok")
        dve_own, pool_own = sem("dve_own"), sem("pool_own")
        stored = sem("stored")
        DVE_OWN, POOL_OWN = 41, 29

        block = ctx.enter_context(nc.Block())

        def qkv_of(g, h, t):
            if g == "B":
                q = qb[:, t, h * (NOPE + ROPE):h * (NOPE + ROPE) + NOPE]
                return q, kvb[:, t, h * 2 * P:h * 2 * P + P], kvb[:, t, h * 2 * P + P:(h + 1) * 2 * P]
            q0, k0, v0 = {"A": (A_Q, A_K, A_V), "C": (C_Q, C_K, C_V), "D": (D_Q, D_K, D_V)}[g]
            kv = h // (C_HEADS // C_KV) if g == "C" else h
            return tuple(qkv[:, t, c + n * P:c + (n + 1) * P] for c, n in ((q0, h), (k0, kv), (v0, kv)))

        def scale_of(g):
            return {"A": 64, "B": NOPE + ROPE, "C": P, "D": P}[g] ** -0.5

        def slab_view(buf, slot, kts, cols):
            return buf[:, slot, 0:kts * cols].rearrange("p (k n) -> p k n", k=kts)

        @block.sync
        def _(sp):
            sp.dma_start(oh_s, onehot_d).then_inc(r_load, 16)
            sp.dma_start(rel_s, rel_d).then_inc(r_load, 16)
            sp.dma_start(lnc_s, lncount_d).then_inc(r_load, 16)
            sp.dma_start(flip, flip_d).then_inc(r_load, 16)
            for t in range(TT):
                sp.dma_start(x[:, t, :], x_d[t]).then_inc(x_load, 16)
            sp.dma_start(ident[:], ident_d).then_inc(c_load, 16)
            sp.dma_start(rope[:], rope_d).then_inc(c_load, 16)
            sp.dma_start(axial[:], axial_d).then_inc(c_load, 16)
            sp.dma_start(small_all[:, :, 0:N_COLS], small_d).then_inc(c_load, 16)
            for la in range(LAYERS):
                sp.dma_start(small_all[:, la, G_CQN:N_SMALL],
                             gqa_d[la:la + 1, :].to_broadcast([P, 2 * P])).then_inc(c_load, 16)
            sp.dma_start(lam_in[:].rearrange("p l f d -> p (l f d)"),
                         lam_d.to_broadcast([P, LAYERS * 256])).then_inc(c_load, 16)

            def load(la, s, src, size=SLAB):
                sp.wait_ge(lo_done, la * SLABS + s + 1)
                sp.dma_start(raw[:, s_slot(s), 0:size], src).then_inc(loaded[s_slot(s)], 16)

            def s_slot(s):
                return s % 2 if isinstance(s, int) else s_par[0]

            s_par = [0]

            def stream(la, w, base, count, first, per_layer):
                with sp.Fori(0, count // 2) as i:
                    for par in range(2):
                        s_par[0] = par
                        load(la, i * 2 + (base + par),
                             w[bass.ds(la * per_layer + i * 2 + (first + par), 1)].rearrange("a p n -> (a p) n"))

            with sp.Fori(0, LAYERS) as la:
                stream(la, w_in, 0, 16, 0, 40)
                at = 0
                for j, size in enumerate(MLA_SIZE):
                    load(la, S_MLA + j, w_mla[bass.ds(la, 1), :, at:at + size].rearrange("a p n -> (a p) n"), size)
                    at += size
                stream(la, w_in, S_MLA + 4, 24, 16, 40)
                stream(la, w_out, S_OUT, 16, 0, 16)
                stream(la, w_gu, S_GU, 4 * GU_CHUNKS, 0, 4 * GU_CHUNKS)
                stream(la, w_dn, S_DN, DN_SLABS, 0, DN_SLABS)
            for c in range(4):
                sp.wait_ge(x_ready, 4 + LAYERS * 8 - 4 + c + 1)
                sp.dma_start(out_d[:, :, c * CH:(c + 1) * CH].rearrange("t p n -> p t n"),
                             x[:, :, c * CH:(c + 1) * CH]).then_inc(stored, 16)
            sp.wait_ge(stored, 64)

        @block.gpsimd
        def _(pool):
            g = nc.gpsimd
            own = [0]
            layer = [0]

            def link(ins):
                own[0] += 1
                ins.then_inc(pool_own, 1)
                pool.wait_ge(pool_own, layer[0] * POOL_OWN + own[0])

            def rstd(out, mean, var, n):
                link(g.tensor_tensor(var, mean, eps_row[:, 0:n], ALU.add))
                return g.tensor_tensor(out, var, mhalf[:, 0:n], ALU.pow)

            for buf, value in ((mhalf[:], -0.5), (eps_row[:], EPS), (inv_head[:], 1.0 / P),
                               (inv_rank[:, 0:2], 1.0 / Q_RANK), (inv_rank[:, 2:4], 1.0 / KV_RANK)):
                g.memset(buf, value).then_inc(set_up, 1)
            pool.wait_ge(set_up, 5)
            pool.wait_ge(c_load, 7 * 16)
            pool.wait_ge(lam_a, 1)
            g.tensor_tensor(lam_d1[:], lam_e[:, :, 0], lam_e[:, :, 1], ALU.subtract).then_inc(set_up, 1)
            pool.wait_ge(set_up, 6)
            g.tensor_tensor(lam_all[:], lam_d1[:], small_all[:, :, LAM0], ALU.add).then_inc(set_up, 1)
            pool.wait_ge(set_up, 7)
            pool.wait_ge(rel_sum, 1)
            g.dma_start(rel_rows, relrow_s).then_inc(rel_out, 16)
            pool.wait_ge(rel_out, 16)
            src = bass.AP(rel_rows.tensor, 0, [[1, P], [512, 8], [1, SEQ + P]])
            g.dma_start(bias_rev, src).then_inc(rel_in, 16)

            with pool.Fori(0, LAYERS) as la:
                layer[0] = la
                own[0] = 0
                pool.wait_ge(x_ready, la * 8 + 4)
                g.tensor_copy(small[:], small_all[:, bass.ds(la, 1), :].rearrange("p a n -> p (a n)")).then_inc(params, 1)
                link(g.tensor_copy(lam[:], lam_all[:, bass.ds(la, 1)]))
                g.tensor_tensor(gsub[:], small[:, G_SUB:G_SUB + 1], small[:, ONE_LAM0:ONE_LAM0 + 1], ALU.mult).then_inc(params, 1)
                pool.wait_ge(xsq, la * 2 + 1)
                rstd(rs[:], xss[:], xvar[:], TT).then_inc(rs_ok, 1)
                lat = qkv[:, :, B_CQ:B_CQ + 768]
                tl = tmp[:].rearrange("p (t n) -> p t n", t=TT)
                pool.wait_ge(acc_free, la * CHUNKS + ORDER["in", 1] + 3)
                g.tensor_tensor(tl, lat, lat, ALU.mult).then_inc(sq_b, 1)
                pool.wait_ge(ss_b, la + 1)
                link(g.tensor_tensor(bmean[:], bss[:], inv_rank[:], ALU.mult))
                rstd(brs[:], bmean[:], bvar[:], 4).then_inc(brs_ok, 1)

                def rotate(x1, x2, cos, sin, t1, t2, t3, t4, done=None):
                    g.tensor_tensor(t1, x1, cos, ALU.mult)
                    g.tensor_tensor(t2, x2, sin, ALU.mult)
                    g.tensor_tensor(t3, x2, cos, ALU.mult)
                    link(g.tensor_tensor(t4, x1, sin, ALU.mult))
                    g.tensor_tensor(x1, t1, t2, ALU.subtract)
                    link(g.tensor_tensor(x2, t3, t4, ALU.add))

                def parts(shape):
                    n = int(np.prod(shape))
                    return [shaped(tmp[:, i * 384:i * 384 + n], shape) for i in range(4)]

                def shaped(ap, shape):
                    if len(shape) == 2:
                        return ap.rearrange("p (a b) -> p a b", a=shape[0])
                    return ap.rearrange("p (a b c) -> p a b c", a=shape[0], b=shape[1])

                kp = qkv[:, :, B_KPE:B_KPE + ROPE]
                rotate(kp[:, :, 0:32], kp[:, :, 32:64], rope[:, :, 0, :], rope[:, :, 1, :], *parts((2, 32)))
                g.sem_inc(kpe_ok, 1)
                pool.wait_ge(acc_free, la * CHUNKS + ORDER["mla", 1] + 3)
                for t in range(TT):
                    qh = qb[:, t, :].rearrange("p (h d) -> p h d", d=NOPE + ROPE)[:, :, NOPE:NOPE + ROPE]
                    cos = rope[:, t, 0, :].unsqueeze(1).to_broadcast([P, 4, 32])
                    sin = rope[:, t, 1, :].unsqueeze(1).to_broadcast([P, 4, 32])
                    rotate(qh[:, :, 0:32], qh[:, :, 32:64], cos, sin, *parts((4, 32)))
                g.sem_inc(bq_ok, 1)
                cqk = qkv[:, :, C_Q:C_Q + 768]
                pool.wait_ge(acc_free, la * CHUNKS + ORDER["in", 3] + 3)
                link(g.tensor_tensor(tl, cqk, cqk, ALU.mult))
                g.sem_inc(sq_c, 1)
                pool.wait_ge(ss_c, la + 1)
                link(g.tensor_tensor(cmean[:], css[:], inv_head[:], ALU.mult))
                link(rstd(crs[:], cmean[:], cvar[:], 12))
                for t in range(TT):
                    heads = cqk[:, t, :].rearrange("p (h d) -> p h d", d=P)
                    ri = crs[:, t * 6:t * 6 + 6].unsqueeze(2).to_broadcast([P, 6, P])
                    link(g.tensor_tensor(heads, heads, ri, ALU.mult))
                    for h0, nh, col in ((0, C_HEADS, G_CQN), (C_HEADS, C_KV, G_CKN)):
                        gain = small[:, col:col + P].unsqueeze(1).to_broadcast([P, nh, P])
                        link(g.tensor_tensor(heads[:, h0:h0 + nh, :], heads[:, h0:h0 + nh, :], gain, ALU.mult))
                for t in range(TT):
                    pair = cqk[:, t, :].rearrange("p (h f w d) -> p h f w d", f=2, w=2, d=32)
                    cos = axial[:, 0, t].unsqueeze(1).to_broadcast([P, 6, 2, 32])
                    sin = axial[:, 1, t].unsqueeze(1).to_broadcast([P, 6, 2, 32])
                    rotate(pair[:, :, :, 0, :], pair[:, :, :, 1, :], cos, sin, *parts((6, 2, 32)))
                g.sem_inc(c_ok, 1)
                pool.wait_ge(ao_ss, la + 1)
                link(g.tensor_tensor(amean[:], ass[:], inv_head[:, 0:8], ALU.mult))
                rstd(ars[:], amean[:], avar[:], 8).then_inc(ao_rs, 1)
                pool.wait_ge(y_sum, la * 2 + 1)
                rstd(rsy[:], ysum[:], yvar[:], TT).then_inc(rsy_ok, 1)
                pool.wait_ge(xsq, la * 2 + 2)
                rstd(rs[:], xss[:], xvar[:], TT).then_inc(rs_ok, 1)
                pool.wait_ge(y_sum, la * 2 + 2)
                rstd(rsy[:], ysum[:], yvar[:], TT).then_inc(rsy_ok, 1)
                if own[0] != POOL_OWN:
                    raise ValueError(f"POOL_OWN = {own[0]}")

        @block.scalar
        def _(act):
            a = nc.scalar
            la_ = [0]

            def hi(s, size=SLAB):
                k, par = s
                act.wait_ge(loaded[par], (la_[0] * (SLABS // 2) + k) * 16 + 16)
                act.wait_ge(used, (la_[0] * (SLABS // 2) + k) * 2 + (par + 1))
                a.activation(w_hi[:, par, 0:size], raw[:, par, 0:size], ACT.Copy).then_inc(hi_done, 1)

            def hx(n):
                col = G_MIX if n == 0 else G_FFN
                for b in range(8):
                    act.wait_ge(hx_tr, (la_[0] * 2 + n) * 8 + b + 1)
                    for kk in range(2):
                        k = 2 * b + kk
                        last = a.activation(h_hi[:, k, :], ps[:, 4 + b % 4, kk * SEQ:(kk + 1) * SEQ],
                                            ACT.Copy, scale=small[:, col + k:col + k + 1])
                    last.then_inc(hx_hi, 1)
                act.wait_ge(x_ready, la_[0] * 8 + (4 * n + 4))
                if n == 1:
                    act.dma_start(gpost, post_ffn[bass.ds(la_[0], 1), :].to_broadcast([P, D])).then_inc(post_load, 16)
                for t in range(TT):
                    last = a.activation(y[:, t, :], x[:, t, :], ACT.Square, scale=D ** -0.5,
                                        accum_out=xss[:, t:t + 1])
                last.then_inc(xsq, 1)

            def y_squares(slabs, banks, quarter, before):
                act.wait_ge(used, slabs)
                act.wait_ge(y_sq, before)
                for t in range(TT):
                    last = a.activation(tmp[:, t * CH:(t + 1) * CH], ps[:, banks + t, :], ACT.Square, scale=D ** -0.5,
                                        accum_out=yss[:, t, quarter])
                last.then_inc(y_sq, 1)

            def front_hi(s):
                hi((s // 2, s % 2), SIZE[s] if s < S_GU else SLAB)

            def take(chunk):
                la, (kind, c), bank = la_[0], chunk, 2 * (ORDER[chunk] % 2)
                if kind == "out":
                    y_squares(la * SLABS + (last_slab(chunk) + 3), bank, slice(c, c + 1), la * 8 + (c + 1))
                    return
                if chunk == ("in", 0):
                    act.wait_ge(rs_ok, la * 2 + 1)
                if chunk == ("mla", 0):
                    act.wait_ge(brs_ok, la + 1)
                act.wait_ge(used, la * SLABS + (last_slab(chunk) + 3))
                for t in range(TT):
                    if kind == "in":
                        at, n = IN_ORDER[c]
                        dst, scale = qkv[:, t, at:at + n], rs[:, t:t + 1]
                    else:
                        n = (512, 256, 512, 512)[c]
                        at = (0, 512, 0, 512)[c]
                        dst = (qb if c < 2 else kvb)[:, t, at:at + n]
                        scale = brs[:, 2 * (c // 2) + t:2 * (c // 2) + t + 1]
                    last = a.activation(dst, ps[:, bank + t, 0:n], ACT.Copy, scale=scale)
                last.then_inc(acc_free, 1)

            def heads_out(g):
                if g == "B":
                    return qb.rearrange("p t (h d) -> p h t d", h=4)[:, :, :, 0:P]
                return qkv[:, :, C_Q:C_Q + 512].rearrange("p t (h d) -> p h t d", h=4)

            def attend(half, late):
                la = la_[0]
                if not late:
                    if half == 2 * S_OUT:
                        act.wait_ge(used, la * SLABS + (S_OUT + 2))
                        act.wait_ge(o_out, la * NU + 8)
                        for n, g in enumerate("BC"):
                            a.activation(h_hi[:, 4 * n:4 * n + 4, :].rearrange("p h (t d) -> p h t d", t=TT),
                                         heads_out(g), ACT.Copy).then_inc(mix_hi, 1)
                    if (i := unit(half, 0)) is not None:
                        g, h = UNITS[i]
                        act.wait_ge(t_done, la * NU + (i + 1))
                        last = a.activation(qkT, ps[:, 4, :], ACT.Copy)
                        if g == "B":
                            last = a.activation(qrT[:], ps[0:64, 6, 0:SEQ], ACT.Copy)
                            if h == 0:
                                last = a.activation(kpeT[:], ps[0:64, 6, SEQ:2 * SEQ], ACT.Copy)
                        last.then_inc(t_out, 1)
                    if (i := unit(half, TURN)) is not None:
                        act.wait_ge(pt_done, la * NU + (i + 1))
                        a.activation(PT, ps[:, 6 + 1, :], ACT.Copy).then_inc(pt_out, 1)
                        if i == NU - 1:
                            act.dma_start(gpost, post_mix[bass.ds(la, 1), :].to_broadcast([P, D])).then_inc(post_load, 16)
                    if half == LATENT_AT:
                        for b in range(3):
                            act.wait_ge(ct_tr, la * 3 + (b + 1))
                            for kk in range(2):
                                k = 2 * b + kk
                                last = a.activation(c_hi[:, k, :], ps[:, 4 + b, kk * SEQ:(kk + 1) * SEQ],
                                                    ACT.Copy, scale=small[:, G_CQ + k:G_CQ + k + 1])
                            last.then_inc(ct_hi, 1)
                    return
                if (i := unit(half, EXP)) is not None:
                    g, h = UNITS[i]
                    act.wait_ge(m_ok, la * NU + (i + 1))
                    for m in range(2 if g == "A" else 1):
                        for t in range(TT):
                            cols = slice(t * SEQ, (t + 1) * SEQ)
                            e = prob[:, i % 2, m, cols]
                            src, scale = (e, 1.0) if g in "AD" else (ps[:, 5, cols], scale_of(g))
                            last = a.activation(e, src, ACT.Exp, bias=nmax[:, i % 2, 2 * m + t:2 * m + t + 1],
                                                scale=scale, accum_out=esum[:, i % 2, 2 * m + t:2 * m + t + 1])
                    last.then_inc(e_done, 1)
                if (i := unit(half, OUT)) is not None:
                    g, h = UNITS[i]
                    act.wait_ge(o_done, la * NU + (i + 1))
                    o = ps[:, 7, 0:SEQ]
                    if g == "D":
                        a.activation(h_hi[:, MIX_AT[g] + h, :], o, ACT.Copy).then_inc(o_hi, 1)
                    else:
                        dst = qkv[:, :, A_Q + h * P:A_Q + (h + 1) * P] if g == "A" else heads_out(g)[:, h]
                        a.activation(dst, o.rearrange("p (t d) -> p t d", t=TT), ACT.Copy).then_inc(o_out, 1)
                if half in A_TURN:
                    b = A_TURN.index(half)
                    act.wait_ge(params, la * 2 + 2)
                    act.wait_ge(ao_tr, la * 2 + (b + 1))
                    k = MIX_AT["A"] + 2 * b
                    a.activation(h_hi[:, k:k + 2, :].rearrange("p k n -> p (k n)"), ps[:, 4, :],
                                 ACT.Copy, scale=gsub[:]).then_inc(ao_hi, 1)

            act.wait_ge(lam_v, 2)
            a.activation(lam_e[:].rearrange("p l f -> p (l f)"), lam_e[:].rearrange("p l f -> p (l f)"),
                         ACT.Exp).then_inc(lam_a, 1)

            for h in range(8):
                act.wait_ge(flip_mm, h + 1)
                a.activation(bias[:, h, :], ps[:, h, 0:SEQ + P], ACT.Copy).then_inc(flip_out, 1)

            with act.Fori(0, LAYERS) as la:
                la_[0] = la
                hi((0, 0))
                hi((0, 1))
                act.wait_ge(params, la * 2 + 1)
                act.wait_ge(x_load, 32)
                hx(0)
                for s in range(S_GU):
                    attend(2 * s, False)
                    if s >= 1:
                        front_hi(s + 1)
                        if s - 1 in ENDED:
                            take(ENDED[s - 1])
                    attend(2 * s, True)
                    attend(2 * s + 1, False)
                    attend(2 * s + 1, True)
                take(("out", 3))
                front_hi(S_GU + 1)
                hx(1)
                act.wait_ge(rs_ok, la * 2 + 2)

                def gu_chunk(n, par, turn):
                    k = n * 2 + S_GU // 2
                    hi((k + 1, 0))
                    hi((k + 1, 1))
                    if turn:
                        turned(n - 1, 1 - par)
                    hi((k + 2, 0))
                    if isinstance(n, int) and n == GU_CHUNKS - 1:
                        act.wait_ge(ht_out, la * GU_CHUNKS + (2 + 2))
                        hid_hi(0, 0)
                        hid_hi(1, 1)
                    hi((k + 2, 1))
                    act.wait_ge(used, la * SLABS + n * 4 + (S_GU + 6))
                    for t in range(TT):
                        last = a.activation(sg[:, par, t, :], ps[:, 2 * par + t, 0:256], ACT.Silu,
                                            scale=rs[:, t:t + 1])
                    last.then_inc(sw_g, 1)

                def turned(n, par):
                    act.wait_ge(ht_tr, la * GU_CHUNKS + n + 1)
                    dst = big[:, bass.ds(n * 512, 512)]
                    a.activation(dst, ps[:, 4 + par, :], ACT.Copy).then_inc(ht_out, 1)

                def hid_hi(j, par):
                    src = big[:, bass.ds(j * 512, 512)]
                    a.activation(c_hi[:, 2 * par:2 * par + 2, :].rearrange("p k n -> p (k n)"), src,
                                 ACT.Copy).then_inc(hid_hi_ok, 1)

                gu_chunk(0, 0, False)
                with act.Fori(0, 10) as i:
                    gu_chunk(i * 2 + 1, 1, True)
                    gu_chunk(i * 2 + 2, 0, True)
                gu_chunk(21, 1, True)
                turned(21, 1)
                def dn(k, par):
                    act.wait_ge(used, (la * (SLABS // 2) + (S_DN // 2) + k) * 2 + (par + 1))

                act.wait_ge(ht_out, la * GU_CHUNKS + (GU_CHUNKS + 2))
                for half in range(2):
                    with act.Fori(0, 10) as i:
                        for par in range(2):
                            dn(i + (1 + 11 * half), par)
                            hid_hi(i * 2 + (2 + par), par)
                            hi((i + (S_DN // 2 + 1 + 11 * half), par))
                    if half == 0:
                        for par in range(2):
                            dn(11, par)
                            hid_hi(par, par)
                            hi((S_DN // 2 + 11, par))
                    for q in range(2):
                        y_squares(la * SLABS + (S_DN + 22 * half + 24), 4 * half + 2 * q, slice(2 * half + q, 2 * half + q + 1),
                                  la * 8 + (5 + 2 * half + q))

        @block.tensor
        def _(pe):
            t_ = nc.tensor
            la_ = [0]

            def split_product(out, k, t, w, wl, first, last, hh=h_hi, hl=h_lo):
                cols = slice(t * P, (t + 1) * P)
                t_.matmul(out, hh[:, k, cols], w, start=first, stop=False)
                t_.matmul(out, hh[:, k, cols], wl, start=False, stop=False)
                return t_.matmul(out, hl[:, k, cols], w, start=False, stop=last)

            def slab_ready(k, par):
                pe.wait_ge(lo_done, (la_[0] * (SLABS // 2) + k) * 2 + (par + 3))

            def chunk(k, c, par, middle=None, h_base=None):
                pe.wait_ge(acc_free, c + 1)
                for j in range(4):
                    pe.wait_ge(hx_lo, h_base + (2 * j + 2))
                    slab_ready(k + j // 2, j % 2)
                    for kk in range(4):
                        kt = 4 * j + kk
                        for t in range(TT):
                            last = split_product(ps[:, 2 * par + t, :], kt, t,
                                                 slab_view(w_hi, j % 2, 4, CH)[:, kk, :],
                                                 slab_view(w_lo, j % 2, 4, CH)[:, kk, :],
                                                 kt == 0, kt == KT - 1)
                    last.then_inc(used, 1)
                    if j == 1 and middle:
                        middle()

            def turn(out, src):
                return t_.transpose(out, src, ident[:])

            def hx(n):
                for b in range(8):
                    if b % 2 == 0:
                        pe.wait_ge(x_ready, la_[0] * 8 + (4 * n + b // 2 + 1))
                    if b >= 4:
                        pe.wait_ge(hx_lo, (la_[0] * 2 + n) * 8 + b - 3)
                    for kk in range(2):
                        for t in range(TT):
                            k = 2 * b + kk
                            last = turn(ps[:, 4 + b % 4, kk * SEQ + t * P:kk * SEQ + (t + 1) * P],
                                        x[:, t, k * P:(k + 1) * P])
                    last.then_inc(hx_tr, 1)

            pe.wait_ge(r_load, 64)
            t_.matmul(ps[0:8, 0, :], rel_s, oh_s, start=True, stop=True).then_inc(rel_mm, 1)
            pe.wait_ge(rel_sum, 1)
            pe.wait_ge(c_load, 7 * 16)
            pe.wait_ge(x_load, 32)

            pe.wait_ge(rel_in, 16)
            for h in range(8):
                t_.matmul(ps[:, h, 0:SEQ + P], flip, bias_rev[:, h, :], start=True, stop=True).then_inc(flip_mm, 1)
            pe.wait_ge(flip_out, 8)

            with pe.Fori(0, LAYERS) as la:
                la_[0] = la
                hx(0)
                def transposes(i):
                    g, h = UNITS[i]
                    if i >= 1:
                        pe.wait_ge(t_out, la * NU + i)
                    if g == "D" and h >= 2:
                        pe.wait_ge(ao_lo, la * 2 + (h - 1))
                    if h == 0:
                        ready = {"B": ("mla", 3), "C": ("in", 3), "A": ("in", 5), "D": ("in", 8)}[g]
                        pe.wait_ge(acc_free, la * CHUNKS + (ORDER[ready] + 3))
                    if g == "C" and h == 0:
                        pe.wait_ge(c_ok, la + 1)
                    if g == "B" and h == 0:
                        pe.wait_ge(bq_ok, la + 1)
                        pe.wait_ge(kpe_ok, la + 1)
                    for t in range(TT):
                        q, k, _ = qkv_of(g, h, t)
                        turn(ps[:, 4, t * P:(t + 1) * P], q)
                        last = turn(ps[:, 4, SEQ + t * P:SEQ + (t + 1) * P], k)
                        if g == "B":
                            at = h * (NOPE + ROPE) + NOPE
                            last = turn(ps[0:64, 6, t * P:(t + 1) * P], qb[:, t, at:at + ROPE])
                            if h == 0:
                                last = turn(ps[0:64, 6, SEQ + t * P:SEQ + (t + 1) * P],
                                            qkv[:, t, B_KPE:B_KPE + ROPE])
                    last.then_inc(t_done, 1)

                def scores(i):
                    g, h = UNITS[i]
                    pe.wait_ge(t_out, la * NU + i + 1)
                    for m in range(2 if g == "A" else 1):
                        rows = slice(64 * m, 64 * m + 64) if g == "A" else slice(0, P)
                        for t in range(TT):
                            out = ps[:, 5 + m, t * SEQ:(t + 1) * SEQ]
                            last = t_.matmul(out, qkT[rows, t * P:(t + 1) * P], qkT[rows, SEQ:2 * SEQ],
                                             start=True, stop=g != "B")
                            if g == "B":
                                last = t_.matmul(out, qrT[:, t * P:(t + 1) * P], kpeT[:], start=False, stop=True)
                    last.then_inc(s_done, 1)

                def prob_transposes(i):
                    pe.wait_ge(p_ok, la * NU + i + 1)
                    if i >= 1:
                        pe.wait_ge(o_out, la * NU + i)
                    for kt in range(TT):
                        for t in range(TT):
                            last = turn(ps[:, 7, kt * SEQ + t * P:kt * SEQ + (t + 1) * P],
                                        prob[:, i % 2, 0, t * SEQ + kt * P:t * SEQ + (kt + 1) * P])
                    last.then_inc(pt_done, 1)

                def outputs(i):
                    g, h = UNITS[i]
                    pe.wait_ge(pt_out, la * NU + i + 1)
                    if g in "AD" and h == 0:
                        pe.wait_ge(acc_free, la * CHUNKS + (ORDER["in", 6 if g == "A" else 9] + 3))
                    pt = PT.rearrange("p (k n) -> p k n", k=TT)
                    if g == "A":
                        for t in range(TT):
                            for kt in range(TT):
                                last = t_.matmul(ps[:, 7, t * P:(t + 1) * P], pt[:, kt, t * P:(t + 1) * P],
                                                 qkv_of(g, h, kt)[2], start=kt == 0, stop=kt == TT - 1)
                    else:
                        for kt in range(TT):
                            last = t_.matmul(ps[:, 7, 0:SEQ], qkv_of(g, h, kt)[2], pt[:, kt, :],
                                             start=kt == 0, stop=kt == TT - 1)
                    last.then_inc(o_done, 1)

                def steps(half):
                    for step, do in ((TURN, prob_transposes), (SCORE, scores), (0, transposes), (OUT, outputs)):
                        if (i := unit(half, step)) is not None:
                            do(i)
                    if half in A_TURN:
                        b = A_TURN.index(half)
                        pe.wait_ge(ao_n, la + 1)
                        i = max(START[f] for f in START if f <= half)
                        pe.wait_ge(t_out, la * NU + (i + 1))
                        if b == 1:
                            pe.wait_ge(ao_lo, la * 2 + 1)
                        for kk in range(2):
                            for t in range(TT):
                                last = turn(ps[:, 4, kk * SEQ + t * P:kk * SEQ + (t + 1) * P],
                                            qkv[:, t, A_Q + (2 * b + kk) * P:A_Q + (2 * b + kk + 1) * P])
                        last.then_inc(ao_tr, 1)
                    if half == LATENT_AT:
                        pe.wait_ge(acc_free, la * CHUNKS + (ORDER["in", 1] + 3))
                        for b in range(3):
                            for kk in range(2):
                                for t in range(TT):
                                    k = 2 * b + kk
                                    last = turn(ps[:, 4 + b, kk * SEQ + t * P:kk * SEQ + (t + 1) * P],
                                                qkv[:, t, B_CQ + k * P:B_CQ + (k + 1) * P])
                            last.then_inc(ct_tr, 1)

                for s, (kind, c, j, n) in enumerate(FRONT):
                    steps(2 * s)
                    order = ORDER[kind, c]
                    if j == 0:
                        pe.wait_ge(acc_free, la * CHUNKS + (order + 1))
                    if (kind, c) == ("in", 0):
                        pe.wait_ge(hx_lo, la * 16 + (2 * j + 2))
                    if kind == "mla":
                        pe.wait_ge(ct_lo, la * 3 + 3)
                    if kind == "out" and c < 2:
                        if j == 3:
                            pe.wait_ge(o_out, la * NU + NU)
                        elif j == 2:
                            pe.wait_ge(ao_lo, la * 2 + 2)
                        else:
                            pe.wait_ge(mix_lo, la * 2 + (j + 1))
                    slab_ready(s // 2, s % 2)
                    kts = SIZE[s] // (n if kind == "mla" else CH)
                    wide = n if kind == "mla" else CH
                    k0 = (0, 0, 4, 4)[c] if kind == "mla" else 4 * j
                    total = {"mla": kts}.get(kind, KT)
                    hh, hl = (c_hi, c_lo) if kind == "mla" else (h_hi, h_lo)
                    for kk in range(kts):
                        if kk == kts // 2:
                            steps(2 * s + 1)
                        for t in range(TT):
                            kt = kk if kind == "mla" else k0 + kk
                            last = split_product(ps[:, 2 * (order % 2) + t, 0:n], k0 + kk, t,
                                                 slab_view(w_hi, s % 2, kts, wide)[:, kk, 0:n],
                                                 slab_view(w_lo, s % 2, kts, wide)[:, kk, 0:n],
                                                 kt == 0, kt == total - 1, hh, hl)
                    last.then_inc(used, 1)
                hx(1)

                def hid_turn(n, par):
                    pe.wait_ge(acc_free, la * CHUNKS + n + (C_GU + 3))
                    pe.wait_ge(ht_out, la * GU_CHUNKS + n + 1)
                    for kk in range(2):
                        for t in range(TT):
                            last = turn(ps[:, 4 + par, kk * SEQ + t * P:kk * SEQ + (t + 1) * P],
                                        act_tile[:, par, t, kk * P:(kk + 1) * P])
                    last.then_inc(ht_tr, 1)

                def gu_chunk(n, par, turned):
                    middle = (lambda: hid_turn(n - 1, 1 - par)) if turned else None
                    chunk(n * 2 + S_GU // 2, la * CHUNKS + n + C_GU, par, middle, h_base=la * 16 + 8)

                gu_chunk(0, 0, False)
                with pe.Fori(0, 10) as i:
                    gu_chunk(i * 2 + 1, 1, True)
                    gu_chunk(i * 2 + 2, 0, True)
                gu_chunk(21, 1, True)

                def dn_slab(k, par, half, first, last):
                    slab_ready(k, par)
                    pe.wait_ge(hid_lo_ok, la * DN_SLABS + (k - S_DN // 2) * 2 + (par + 1))
                    for q in range(2):
                        if first and half == 0:
                            pe.wait_ge(acc_free, la * CHUNKS + (C_DN + 1 + q))
                        for kk in range(2):
                            for t in range(TT):
                                w = slab_view(w_hi, par, 2, 1024)[:, kk, q * CH:(q + 1) * CH]
                                wl = slab_view(w_lo, par, 2, 1024)[:, kk, q * CH:(q + 1) * CH]
                                mm = split_product(ps[:, 4 * half + 2 * q + t, :], 2 * par + kk, t, w, wl,
                                                   first and kk == 0, last and kk == 1, c_hi, c_lo)
                    mm.then_inc(used, 1)

                for half in range(2):
                    k = S_DN // 2 + 11 * half
                    if half == 1:
                        pe.wait_ge(ht_out, la * GU_CHUNKS + (GU_CHUNKS + 2))
                    dn_slab(k, 0, half, True, False)
                    if half == 0:
                        hid_turn(21, 1)
                    dn_slab(k, 1, half, False, False)
                    with pe.Fori(0, 9) as i:
                        for par in range(2):
                            dn_slab(i + (k + 1), par, half, False, False)
                    dn_slab(k + 10, 0, half, False, False)
                    dn_slab(k + 10, 1, half, False, True)

        @block.vector
        def _(dve):
            v = nc.vector
            la_ = [0]
            own = [0]

            def link(ins):
                own[0] += 1
                ins.then_inc(dve_own, 1)
                dve.wait_ge(dve_own, la_[0] * DVE_OWN + own[0])

            def lo(s, size=SLAB):
                k, par = s
                dve.wait_ge(hi_done, (la_[0] * (SLABS // 2) + k) * 2 + (par + 1))
                v.tensor_tensor(w_lo[:, par, 0:size], raw[:, par, 0:size], w_hi[:, par, 0:size].bitcast(F32),
                                ALU.subtract).then_inc(lo_done, 1)

            def hx_b(n, b):
                col = G_MIX if n == 0 else G_FFN
                dve.wait_ge(hx_hi, (la_[0] * 2 + n) * 8 + (b + 1))
                for kk in range(2):
                    k = 2 * b + kk
                    last = v.scalar_tensor_tensor(h_lo[:, k, :], ps[:, 4 + b % 4, kk * SEQ:(kk + 1) * SEQ],
                                                  small[:, col + k:col + k + 1], h_hi[:, k, :].bitcast(F32),
                                                  ALU.mult, ALU.subtract)
                last.then_inc(hx_lo, 1)

            def y_gain(sq, bank, cols, n):
                dve.wait_ge(post_load, la_[0] * 32 + (16 + 16 * n))
                dve.wait_ge(y_sq, sq)
                for t in range(TT):
                    last = v.tensor_tensor(y[:, t, cols], ps[:, bank + t, :], gpost[:, cols], ALU.mult)
                last.then_inc(acc_free, 1)

            def x_update(n):
                v.tensor_reduce(ysum[:], yss[:], AX_X, ALU.add).then_inc(y_sum, 1)
                dve.wait_ge(rsy_ok, la_[0] * 2 + n + 1)
                dve.wait_ge(acc_free, la_[0] * CHUNKS + (C_GU + 2 if n == 0 else CHUNKS + 2))
                if n == 1:
                    for c in range(4):
                        quarter(c)
                    return
                quarter(0)
                quarter(1)
                hx_b(1, 0)
                hx_b(1, 1)
                front_lo(S_GU + 1)
                quarter(2)
                hx_b(1, 2)
                hx_b(1, 3)
                quarter(3)
                for b in range(4, 8):
                    hx_b(1, b)

            def quarter(c):
                cols = slice(c * CH, (c + 1) * CH)
                for t in range(TT):
                    last = v.scalar_tensor_tensor(x[:, t, cols], y[:, t, cols], rsy[:, t:t + 1], x[:, t, cols],
                                                  ALU.mult, ALU.add)
                last.then_inc(x_ready, 1)

            def front_lo(s):
                lo((s // 2, s % 2), SIZE[s] if s < S_GU else SLAB)

            dve.sem_inc(lo_done, 2)
            dve.sem_inc(used, 2)
            dve.sem_inc(acc_free, 2)
            dve.sem_inc(x_ready, 4)
            dve.sem_inc(ht_out, 2)
            dve.sem_inc(y_sq, 1)
            dve.wait_ge(c_load, 7 * 16)
            for la in range(LAYERS):
                for f in range(2):
                    last = v.tensor_tensor(lam_prod[:, 2 * la + f, :], lam_in[:, la, 2 * f, :],
                                           lam_in[:, la, 2 * f + 1, :], ALU.mult)
            last.then_inc(lam_v, 1)
            dve.wait_ge(lam_v, 1)
            v.tensor_reduce(lam_e[:].rearrange("p l f -> p (l f)"), lam_prod[:], AX_X, ALU.add).then_inc(lam_v, 1)
            dve.wait_ge(rel_mm, 1)
            v.tensor_tensor(relrow_s, ps[0:8, 0, :], lnc_s, ALU.add).then_inc(rel_sum, 1)
            dve.wait_ge(x_load, 32)

            with dve.Fori(0, LAYERS) as la:
                la_[0] = la
                own[0] = 0
                dve.wait_ge(params, la * 2 + 1)
                for b in range(8):
                    hx_b(0, b)
                    if b == 1:
                        lo((0, 0))
                    if b == 3:
                        lo((0, 1))
                def softmax_max(i):
                    g, h = UNITS[i]
                    b = i % 2
                    dve.wait_ge(s_done, la * NU + i + 1)
                    if g in "AD":
                        maps = 2 if g == "A" else 1
                        for m in range(maps):
                            for t in range(TT):
                                cols = slice(t * SEQ, (t + 1) * SEQ)
                                at = (1 - t) * P
                                last = v.scalar_tensor_tensor(prob[:, b, m, cols], ps[:, 5 + m, cols], scale_of(g),
                                                              bias[:, (0 if g == "A" else 4) + h, at:at + SEQ],
                                                              ALU.mult, ALU.add)
                        link(last)
                        v.tensor_reduce(nmax[:, b, 0:2 * maps],
                                        prob[:, b, 0:maps, :].rearrange("p m (t n) -> p (m t) n", t=TT),
                                        AX_X, ALU.max, negate=True).then_inc(m_ok, 1)
                    else:
                        link(v.tensor_reduce(mx[:, b, 0:2], ps[:, 5, :].rearrange("p (t n) -> p t n", t=TT),
                                             AX_X, ALU.max))
                        v.tensor_scalar(nmax[:, b, 0:2], mx[:, b, 0:2], -scale_of(g), None, ALU.mult).then_inc(m_ok, 1)

                def softmax_norm(i):
                    g, h = UNITS[i]
                    b = i % 2
                    dve.wait_ge(e_done, la * NU + i + 1)
                    if g == "A":
                        link(v.reciprocal(rsum[:, b, :], esum[:, b, :]))
                        link(v.tensor_scalar(rlam[:, b, :], rsum[:, b, 2:4], lam[:], None, ALU.mult))
                        for t in range(TT):
                            cols = slice(t * SEQ, (t + 1) * SEQ)
                            last = v.tensor_scalar(prob[:, b, 1, cols], prob[:, b, 1, cols], rlam[:, b, t:t + 1],
                                                   None, ALU.mult)
                        link(last)
                    else:
                        link(v.reciprocal(rsum[:, b, 0:2], esum[:, b, 0:2]))
                    for t in range(TT):
                        cols = slice(t * SEQ, (t + 1) * SEQ)
                        if g == "A":
                            last = v.scalar_tensor_tensor(prob[:, b, 0, cols], prob[:, b, 0, cols],
                                                          rsum[:, b, t:t + 1], prob[:, b, 1, cols],
                                                          ALU.mult, ALU.subtract)
                        else:
                            last = v.tensor_scalar(prob[:, b, 0, cols], prob[:, b, 0, cols], rsum[:, b, t:t + 1],
                                                   None, ALU.mult)
                    last.then_inc(p_ok, 1)

                def attend(half, late):
                    if not late:
                        if (i := unit(half, SCORE)) is not None:
                            softmax_max(i)
                        if half == 2 * S_OUT:
                            for n, src in enumerate((qb.rearrange("p t (h d) -> p h t d", h=4)[:, :, :, 0:P],
                                                     qkv[:, :, C_Q:C_Q + 512].rearrange("p t (h d) -> p h t d", h=4))):
                                dve.wait_ge(mix_hi, la * 2 + (n + 1))
                                for h in range(4):
                                    k = 4 * n + h
                                    last = v.tensor_tensor(h_lo[:, k, :].rearrange("p (t d) -> p t d", t=TT), src[:, h],
                                                           h_hi[:, k, :].bitcast(F32).rearrange("p (t d) -> p t d", t=TT),
                                                           ALU.subtract)
                                last.then_inc(mix_lo, 1)
                        return
                    if (i := unit(half, EXP)) is not None:
                        softmax_norm(i)
                    i = unit(half, OUT)
                    if i is not None and UNITS[i][0] == "D":
                        k = MIX_AT["D"] + UNITS[i][1]
                        dve.wait_ge(o_hi, la * 4 + (UNITS[i][1] + 1))
                        v.tensor_tensor(h_lo[:, k, :], ps[:, 7, 0:SEQ], h_hi[:, k, :].bitcast(F32),
                                        ALU.subtract).then_inc(o_out, 1)
                    if half == LATENT_AT:
                        for b in range(3):
                            dve.wait_ge(ct_hi, la * 3 + (b + 1))
                            for kk in range(2):
                                k = 2 * b + kk
                                last = v.scalar_tensor_tensor(c_lo[:, k, :], ps[:, 4 + b, kk * SEQ:(kk + 1) * SEQ],
                                                              small[:, G_CQ + k:G_CQ + k + 1],
                                                              c_hi[:, k, :].bitcast(F32), ALU.mult, ALU.subtract)
                            last.then_inc(ct_lo, 1)
                    tl = tmp[:].rearrange("p (t n) -> p t n", t=TT)
                    if half == LATENT_AT + 2:
                        dve.wait_ge(sq_b, la + 1)
                        v.tensor_reduce(bss[:, 0:2], tl[:, :, 0:Q_RANK], AX_X, ALU.add)
                        v.tensor_reduce(bss[:, 2:4], tl[:, :, Q_RANK:768], AX_X, ALU.add).then_inc(ss_b, 1)
                    if half == SQ_C_AT:
                        dve.wait_ge(sq_c, la + 1)
                        v.tensor_reduce(css[:], tmp[:].rearrange("p (g d) -> p g d", d=P), AX_X,
                                        ALU.add).then_inc(ss_c, 1)
                    if half == A_SQUARE:
                        dve.wait_ge(o_out, la * NU + 12)
                        link(v.tensor_tensor(qkv[:, :, A_K:A_K + 512], qkv[:, :, A_Q:A_Q + 512],
                                             qkv[:, :, A_Q:A_Q + 512], ALU.mult))
                        for t in range(TT):
                            last = v.tensor_reduce(ass[:, 4 * t:4 * t + 4],
                                                   qkv[:, t, A_K:A_K + 512].rearrange("p (h d) -> p h d", d=P),
                                                   AX_X, ALU.add)
                        last.then_inc(ao_ss, 1)
                    if half == A_NORM:
                        dve.wait_ge(ao_rs, la + 1)
                        for t in range(TT):
                            o = qkv[:, t, A_Q:A_Q + 512].rearrange("p (h d) -> p h d", d=P)
                            last = v.tensor_tensor(o, o, ars[:, 4 * t:4 * t + 4].unsqueeze(2).to_broadcast([P, 4, P]),
                                                   ALU.mult)
                        last.then_inc(ao_n, 1)
                    if half in A_TURN:
                        n = A_TURN.index(half)
                        k = MIX_AT["A"] + 2 * n
                        dve.wait_ge(ao_hi, la * 2 + (n + 1))
                        v.scalar_tensor_tensor(h_lo[:, k:k + 2, :].rearrange("p k n -> p (k n)"), ps[:, 4, :], gsub[:],
                                               h_hi[:, k:k + 2, :].rearrange("p k n -> p (k n)").bitcast(F32),
                                               ALU.mult, ALU.subtract).then_inc(ao_lo, 1)

                def out_gain(c):
                    y_gain(la * 8 + (c + 2), 2 * (ORDER["out", c] % 2), slice(c * CH, (c + 1) * CH), 0)

                dve.wait_ge(flip_out, 8)
                for s in range(S_GU):
                    attend(2 * s, False)
                    if s >= 1:
                        front_lo(s + 1)
                        if ENDED.get(s - 1, ("", 0))[0] == "out":
                            out_gain(ENDED[s - 1][1])
                    attend(2 * s, True)
                    attend(2 * s + 1, False)
                    attend(2 * s + 1, True)
                out_gain(3)
                x_update(0)

                def hid_lo(j, par, count):
                    dve.wait_ge(hid_hi_ok, count)
                    src = big[:, bass.ds(j * 512, 512)]
                    hh = c_hi[:, 2 * par:2 * par + 2, :].rearrange("p k n -> p (k n)").bitcast(F32)
                    v.tensor_tensor(c_lo[:, 2 * par:2 * par + 2, :].rearrange("p k n -> p (k n)"), src, hh,
                                    ALU.subtract).then_inc(hid_lo_ok, 1)

                base = la * 44

                def gu_chunk(n, par, at_end=False):
                    k = n * 2 + S_GU // 2
                    lo((k + 1, 0))
                    lo((k + 1, 1))
                    lo((k + 2, 0))
                    if at_end:
                        hid_lo(0, 0, base + 1)
                        hid_lo(1, 1, base + 2)
                    lo((k + 2, 1))
                    dve.wait_ge(sw_g, la * GU_CHUNKS + n + 1)
                    for t in range(TT):
                        last = v.scalar_tensor_tensor(act_tile[:, par, t, :], ps[:, 2 * par + t, 256:512],
                                                      rs[:, t:t + 1], sg[:, par, t, :], ALU.mult, ALU.mult)
                    last.then_inc(acc_free, 1)

                with dve.Fori(0, GU_CHUNKS // 2 - 1) as i:
                    gu_chunk(i * 2, 0)
                    gu_chunk(i * 2 + 1, 1)
                gu_chunk(GU_CHUNKS - 2, 0)
                gu_chunk(GU_CHUNKS - 1, 1, True)

                for half in range(2):
                    with dve.Fori(0, 10) as i:
                        for par in range(2):
                            hid_lo(i * 2 + (2 + par), par, base + i * 2 + (22 * half + 3 + par))
                            lo((i + (S_DN // 2 + 1 + 11 * half), par))
                    if half == 0:
                        for par in range(2):
                            hid_lo(par, par, base + 22 + par + 1)
                            lo((S_DN // 2 + 11, par))
                    for q in range(2):
                        y_gain(la * 8 + (4 + 2 * half + q + 2), 4 * half + 2 * q,
                               slice((2 * half + q) * CH, (2 * half + q + 1) * CH), 1)
                x_update(1)
                if own[0] != DVE_OWN:
                    raise ValueError(f"DVE_OWN = {own[0]}")


def constants():
    rel = np.arange(511) - 255
    n = np.abs(rel)
    nf = np.maximum(n, 8).astype(np.float32)
    large = 8 + (np.log(nf / np.float32(8)) / np.float32(np.log(1024 / 8)) * np.float32(8)).astype(np.int32)
    bucket = np.where(rel > 0, 16, 0) + np.where(n < 8, n, np.minimum(large, 15))
    onehot = np.zeros((32, 512), np.float32)
    onehot[bucket, np.arange(511)] = 1.0
    count = np.zeros(511)
    for w, r in ((128, 1), (512, 4), (2048, 16)):
        count += (n <= w // 2) & (n % r == 0)
    lncount = np.zeros((8, 512), np.float32)
    lncount[4:, :511] = np.where(count > 0, np.log(np.maximum(count, 1)), -1e30)
    pos = np.arange(SEQ)

    def angles(p, dim):
        inv = (np.float32(10000.0) ** (-np.arange(0, dim, 2, dtype=np.float32) / np.float32(dim))).astype(np.float32)
        ang = (p.astype(np.float32)[:, None] * inv[None, :]).astype(np.float32).astype(np.float64)
        return np.stack([np.cos(ang), np.sin(ang)]).astype(np.float32)

    rope = angles(pos, 64).reshape(2, TT, P, 32).transpose(2, 1, 0, 3)
    ax = np.stack([angles(pos // 64, 64), angles(pos % 64, 64)], 1)
    axial = ax.reshape(2, 2, TT, P, 32).transpose(3, 0, 2, 1, 4)
    return {"onehot_d": onehot, "lncount_d": lncount, "ident_d": np.eye(P, dtype=np.float32), "flip_d": np.eye(P, dtype=np.float32)[::-1],
            "rope_d": np.ascontiguousarray(rope), "axial_d": np.ascontiguousarray(axial)}


def lay_out(v):
    L = LAYERS
    asc = np.ascontiguousarray
    w = v["w_in"]
    pad = np.zeros((L, D, PAD), np.float32)
    w = np.concatenate([w[:, :, :PAD_AT], pad, w[:, :, PAD_AT:]], 2)
    slabs = lambda m, c: m.reshape(L, 4, 4, P, c, CH).transpose(0, 4, 1, 3, 2, 5).reshape(L, c, 4, P, SLAB)
    w_in = slabs(w, 10)[:, [at // CH for at, _ in IN_ORDER]].reshape(L * 40, P, SLAB)
    w_out = v["w_out"].reshape(L, 4, 512, D)[:, [1, 2, 0, 3]].reshape(L, D, D)
    w_out = slabs(w_out, 4).reshape(L, 16, P, SLAB)
    w_out = w_out[:, [4 * c + j for kind, c, j, _ in FRONT if kind == "out"]].reshape(L * 16, P, SLAB)
    gu = v["w_gate_up"].reshape(L, 4, 4, P, 2, GU_CHUNKS, 256).transpose(0, 5, 1, 3, 2, 4, 6)
    dn = v["w_down"].reshape(L, 22, 2, P, 2, 1024).transpose(0, 4, 1, 3, 2, 5)
    uq = v["mla_w_uq"].reshape(L, 4, P, 768).transpose(0, 2, 1, 3)
    ukv = v["mla_w_ukv"].reshape(L, 2, P, 1024).transpose(0, 2, 1, 3)
    mla = np.concatenate([m.reshape(L, P, -1) for m in (uq[..., :512], uq[..., 512:], ukv[..., :512], ukv[..., 512:])], 2)
    col = lambda m: m.reshape(L, -1, P).transpose(2, 0, 1)
    lam0 = [0.8 - 0.6 * np.exp(-0.3 * n) for n in range(L)]
    const = np.broadcast_to(np.array([[a, 1.0 - a] for a in lam0], np.float32), (P, L, 2))
    small = np.concatenate([col(v[n]) for n in ("norm_mix_pre", "norm_ffn_pre", "mla_q_norm", "mla_kv_norm", "diff_subln")]
                           + [const], 2)
    arrays = {
        "x_d": v["x"].reshape(TT, P, D), "w_in": w_in, "w_mla": mla,
        "w_out": w_out, "w_gu": gu.reshape(L * GU_CHUNKS * 4, P, SLAB),
        "w_dn": dn.reshape(L * DN_SLABS, P, SLAB), "small_d": small,
        "gqa_d": np.concatenate([v["gqa_q_norm"], v["gqa_k_norm"]], 1),
        "post_mix": v["norm_mix_post"], "post_ffn": v["norm_ffn_post"],
        "lam_d": v["diff_lambda"].reshape(1, -1), "rel_d": v["rel_bias"],
    }
    arrays.update(constants())
    return {n: asc(m) for n, m in arrays.items()}


def kernel(**inputs):
    import concourse.bacc as bacc
    from concourse.bass_utils import run_bass_kernel_spmd

    nc = bacc.Bacc("TRN2", target_bir_lowering=False, num_devices=1)
    arrays = lay_out({n: np.asarray(m) for n, m in inputs.items()})
    args = {n: nc.dram_tensor(n, m.shape, mybir.dt.from_np(m.dtype), kind="ExternalInput").ap()
            for n, m in arrays.items()}
    out = nc.dram_tensor("out_d", (TT, P, D), F32, kind="ExternalOutput").ap()
    build(nc, out_d=out, **args)
    r = run_bass_kernel_spmd(nc, [arrays], core_ids=[0])
    return r.results[0]["out_d"].reshape(1, SEQ, D)
```

```python
from contextlib import ExitStack

import numpy as np
import concourse.bass as bass
from concourse import mybir
from concourse.alu_op_type import AluOpType as ALU

F32 = mybir.dt.float32
F32R = mybir.dt.float32r
ACT = mybir.ActivationFunctionType
AX_X = mybir.AxisListType.X

P = 128
LAYERS, D, SEQ = 2, 2048, 256
TT = SEQ // P
KT = D // P
HID = 5632
EPS = 1e-6
SLAB = 2048
CH = 512

A_Q, A_K, A_V, B_CQ, B_CKV, B_KPE = 0, 512, 1024, 1536, 2048, 2304
C_Q, C_K, C_V, D_Q, D_K, D_V = 2560, 3072, 3328, 3584, 4096, 4608
PAD_AT, PAD = 2368, 192
IN_COLS = 4928
Q_RANK, KV_RANK, NOPE, ROPE = 512, 256, 128, 64
C_HEADS, C_KV = 4, 2

IN_ORDER = ((B_CQ, 512), (B_CKV, 320), (C_Q, 512), (C_K, 512),
            (A_Q, 512), (A_K, 512), (A_V, 512), (D_Q, 512), (D_K, 512), (D_V, 512))
MLA_SIZE = (2048, 1024, 2048)
GU_CHUNKS, DN_SLABS = 22, 44

def quarter_of(kind, c, j):
    return [(kind, c, 4 * j, 4, CH)]


FRONT = [quarter_of("in", 0, j) for j in range(4)]
FRONT += [[("in", 1, k0, n, IN_ORDER[1][1])] for k0, n in ((0, 6), (6, 6), (12, 4))]
FRONT += [quarter_of("in", c, j) for c in (2, 3) for j in range(4)]
S_MLA = len(FRONT)
FRONT += [[("mla", 0, 0, 4, 512)], [("mla", 1, 0, 4, 256)], [("mla", 2, 4, 2, 512), ("mla", 3, 4, 2, 512)]]
FRONT += [quarter_of("in", c, j) for c in range(4, 10) for j in range(4)]
S_OUT = len(FRONT)
FRONT += [quarter_of("out", c, j) for c in range(2) for j in range(3)]
FRONT += [quarter_of("out", 0, 3), quarter_of("out", 1, 3)]
FRONT += [quarter_of("out", c, j) for c in range(2, 4) for j in range(4)]
IN_SLABS = 39
S_GU = len(FRONT)
S_DN = S_GU + 4 * GU_CHUNKS
SLABS = S_DN + DN_SLABS
SIZE = [sum(n * width for *_, n, width in pieces) for pieces in FRONT]

ENDS = [("in", c) for c in range(4)] + [("mla", j) for j in range(4)] + [("in", c) for c in range(4, 10)]
ENDS += [("out", c) for c in range(4)]
C_GU = len(ENDS)
C_DN = C_GU + GU_CHUNKS
CHUNKS = C_DN + 4
ORDER = {e: n for n, e in enumerate(ENDS)}


def last_slab(chunk):
    return max(s for s, pieces in enumerate(FRONT) if chunk in [f[:2] for f in pieces])


ENDED = {last_slab(e): e for e in ENDS}

G_FFN, G_CQ, G_CKV, G_SUB, LAM0, ONE_LAM0 = 0, 16, 20, 22, 23, 24
N_COLS = 25
G_CQN, G_CKN = N_COLS, N_COLS + P
N_SMALL = N_COLS + 2 * P

UNITS = [(g, h) for g in "BCAD" for h in range(4)]
NU = len(UNITS)
FIRST = {"B": 39, "C": 51, "A": 63, "D": 80}
START = {FIRST[g] + 3 * h: u for u, (g, h) in enumerate(UNITS)}
SCORE, EXP, TURN, OUT = 1, 2, 4, 5
REL = 2 * SEQ - 1
LATENT_AT = 18
SQ_C_AT = 42
A_SQUARE, A_NORM, A_TURN = 78, 82, (84, 87)
MIX_AT = {"B": 0, "C": 4, "A": 8, "D": 12}


EARLY = 6


def unit(half, step):
    return START.get(half - step)




def build(nc, x_d, w_in, w_mla, w_out, w_gu, w_dn, small_d, gain_d, gqa_d, post_mix, post_ffn, lam_d, rel_d,
          ident_d, rope_d, axial_d, out_d):
    ctx = ExitStack()
    with ctx:
        def sb(name, shape, dt=F32):
            return ctx.enter_context(nc.sbuf_tensor(name, shape, dt))

        def sem(name):
            return ctx.enter_context(nc.semaphore(name))

        ps = ctx.enter_context(nc.psum_tensor("ps", [P, 8, CH], F32))
        rel_rows = nc.dram_tensor("rel_rows", (8, P * REL), F32, kind="Internal").ap()

        x = sb("x", [P, TT, D])
        y = sb("y", [P, TT, D])
        h_hi = sb("h_hi", [P, KT, SEQ], F32R)
        h_lo = sb("h_lo", [P, KT, SEQ], F32R)
        big = sb("big", [P, 44 * SEQ])
        qkv = big[:, 0:TT * 5120].rearrange("p (t n) -> p t n", t=TT)
        hid = big[:, :].rearrange("p (k n) -> p k n", k=44)
        raw = sb("raw", [P, 2, SLAB])
        w_hi = sb("w_hi", [P, 2, SLAB], F32R)
        w_lo = sb("w_lo", [P, 2, SLAB], F32R)
        bias = sb("bias", [P, 8, SEQ + P])
        c_hi = sb("c_hi", [P, 6, SEQ], F32R)
        c_lo = sb("c_lo", [P, 6, SEQ], F32R)
        work = sb("work", [P, 3072])
        qkT = work[:, 0:512]
        PT = work[:, 512:1024]
        prob = work[:, 1024:3072].rearrange("p (b m n) -> p b m n", b=2, m=2)
        gpost = work[:, 1024:3072]
        y_flat = y[:].rearrange("p t n -> p (t n)")
        sg = y_flat[:, 0:1024].rearrange("p (b t n) -> p b t n", b=2, t=TT)
        act_tile = y_flat[:, 1024:2048].rearrange("p (b t n) -> p b t n", b=2, t=TT)
        qrT = sb("qrT", [64, SEQ])
        kpeT = sb("kpeT", [64, SEQ])
        tmp = sb("tmp", [P, 1536])
        ident = sb("ident", [P, P])
        rope = sb("rope", [P, TT, 2, 32])
        axial = sb("axial", [P, 2, TT, 2, 32])
        gain_all = sb("gain_all", [P, LAYERS, KT])
        small_all = sb("small_all", [P, LAYERS, N_SMALL])
        small = sb("small", [P, N_SMALL])
        g_mix = sb("g_mix", [P, KT])
        lam_in = work[:, 0:LAYERS * 256].rearrange("p (l f d) -> p l f d", l=LAYERS, f=4)
        lam_prod = sb("lam_prod", [P, LAYERS * 2, 64])
        lam_e = sb("lam_e", [P, LAYERS, 2])
        lam_d1 = sb("lam_d1", [P, LAYERS])
        lam_all = sb("lam_all", [P, LAYERS])
        lam = sb("lam", [P, 1])
        gsub = sb("gsub", [P, 1])
        mhalf = sb("mhalf", [P, 12])
        eps_row = sb("eps_row", [P, 12])
        inv_head = sb("inv_head", [P, 12])
        inv_rank = sb("inv_rank", [P, 4])
        xss = sb("xss", [P, TT])
        xvar = sb("xvar", [P, TT])
        rs = sb("rs", [P, TT])
        yss = sb("yss", [P, TT, 5])
        ysum = sb("ysum", [P, TT])
        rsy = sb("rsy", [P, TT])
        bss = sb("bss", [P, 4])
        bmean = sb("bmean", [P, 4])
        bvar = sb("bvar", [P, 4])
        brs = sb("brs", [P, 4])
        css = sb("css", [P, 12])
        cmean = sb("cmean", [P, 12])
        cvar = sb("cvar", [P, 12])
        crs = sb("crs", [P, 12])
        ass = sb("ass", [P, 8])
        amean = sb("amean", [P, 8])
        avar = sb("avar", [P, 8])
        ars = sb("ars", [P, 8])
        mx = sb("mx", [P, 2, 4])
        nmax = sb("nmax", [P, 2, 4])
        esum = sb("esum", [P, 2, 4])
        rsum = sb("rsum", [P, 2, 4])
        rlam = sb("rlam", [P, 2, 2])
        rel_pack = tmp[0:32, 0:512 + 8 + 512]
        oh_s = tmp[0:32, 0:512]
        rel_s = tmp[0:32, 512:520]
        lnc_s = tmp[0:8, 520:1032]
        relrow_s = tmp[0:8, 0:512]
        heads_out = qkv[:, :, C_Q:C_Q + 512].rearrange("p t (h d) -> p h t d", h=4)
        qb = y[:, :, 0:768]
        kvb = y[:, :, 768:1792]

        loaded = [sem("loaded0"), sem("loaded1")]
        hi_done = sem("hi_done")
        lo_done = sem("lo_done")
        used = sem("used")
        acc_free = sem("acc_free")
        x_load = [sem(f"x_load{c}") for c in range(4)]
        i_load, s_load, l_load = sem("i_load"), sem("s_load"), sem("l_load")
        x_ready = sem("x_ready")
        c_load = sem("c_load")
        r_load = sem("r_load")
        rel_mm, rel_sum, rel_out, rel_in = sem("rel_mm"), sem("rel_sum"), sem("rel_out"), sem("rel_in")
        y_g1, y_g0 = sem("y_g1"), sem("y_g0")
        set_up = sem("set_up")
        lam_v, lam_a = sem("lam_v"), sem("lam_a")
        gain_ok = sem("gain_ok")
        params = sem("params")
        hx_tr, hx_hi, hx_lo = sem("hx_tr"), sem("hx_hi"), sem("hx_lo")
        xsq, rs_ok = sem("xsq"), sem("rs_ok")
        post_load = sem("post_load")
        y_sq, y_sum, rsy_ok = sem("y_sq"), sem("y_sum"), sem("rsy_ok")
        sq_b, sq_c, ss_b, ss_c = sem("sq_b"), sem("sq_c"), sem("ss_b"), sem("ss_c")
        brs_ok, kpe_ok, c_ok, bq_ok = sem("brs_ok"), sem("kpe_ok"), sem("c_ok"), sem("bq_ok")
        ct_tr, ct_hi, ct_lo = sem("ct_tr"), sem("ct_hi"), sem("ct_lo")
        t_done, t_out = sem("t_done"), sem("t_out")
        s_done, m_ok, e_done, p_ok = sem("s_done"), sem("m_ok"), sem("e_done"), sem("p_ok")
        pt_done, pt_out = sem("pt_done"), sem("pt_out")
        o_done, o_hi, o_out = sem("o_done"), sem("o_hi"), sem("o_out")
        ao_ss, ao_rs, ao_n, ao_tr, ao_hi, ao_lo = (sem(n) for n in ("ao_ss", "ao_rs", "ao_n", "ao_tr", "ao_hi", "ao_lo"))
        dn_first = sem("dn_first")
        sw_g = sem("sw_g")
        ht_tr = sem("ht_tr")
        ht_out = sem("ht_out")
        mla_mid = sem("mla_mid")
        mix_hi, mix_lo = sem("mix_hi"), sem("mix_lo")
        hid_hi_ok, hid_lo_ok = sem("hid_hi_ok"), sem("hid_lo_ok")
        dve_own, pool_own = sem("dve_own"), sem("pool_own")
        stored = sem("stored")
        DVE_OWN, POOL_OWN = 41, 27

        block = ctx.enter_context(nc.Block())

        def heads_hi_lo(k):
            return (c_hi, c_lo) if k < EARLY else (h_hi, h_lo)

        def qkv_of(g, h, t):
            if g == "B":
                q = qb[:, t, h * (NOPE + ROPE):h * (NOPE + ROPE) + NOPE]
                return q, kvb[:, t, h * 2 * P:h * 2 * P + P], kvb[:, t, h * 2 * P + P:(h + 1) * 2 * P]
            q0, k0, v0 = {"A": (A_Q, A_K, A_V), "C": (C_Q, C_K, C_V), "D": (D_Q, D_K, D_V)}[g]
            kv = h // (C_HEADS // C_KV) if g == "C" else h
            return tuple(qkv[:, t, c + n * P:c + (n + 1) * P] for c, n in ((q0, h), (k0, kv), (v0, kv)))

        def scale_of(g):
            return {"A": 64, "B": NOPE + ROPE, "C": P, "D": P}[g] ** -0.5

        def slab_view(buf, slot, kts, cols):
            return buf[:, slot, 0:kts * cols].rearrange("p (k n) -> p k n", k=kts)

        @block.sync
        def _(sp):
            sp.dma_start(x[:, :, 0:CH], x_d[:, :, 0:CH].rearrange("t p n -> p t n")).then_inc(x_load[0], 16)
            sp.dma_start(rel_pack, rel_d).then_inc(r_load, 16)
            sp.dma_start(gain_all[:], gain_d).then_inc(s_load, 16)

            def load(la, s, src, size=SLAB):
                sp.wait_ge(lo_done, la * SLABS + s + 1)
                sp.dma_start(raw[:, s_slot(s), 0:size], src).then_inc(loaded[s_slot(s)], 16)

            def s_slot(s):
                return s % 2 if isinstance(s, int) else s_par[0]

            s_par = [0]

            def stream(la, w, base, count, first, per_layer):
                with sp.Fori(0, count // 2) as i:
                    for par in range(2):
                        s_par[0] = par
                        load(la, i * 2 + (base + par),
                             w[bass.ds(la * per_layer + i * 2 + (first + par), 1)].rearrange("a p n -> (a p) n"))

            with sp.Fori(0, LAYERS) as la:
                stream(la, w_in, 0, 4, 0, IN_SLABS)

                def load_in(s):
                    load(la, s, w_in[bass.ds(la * IN_SLABS + s, 1), :, 0:SIZE[s]].rearrange("a p n -> (a p) n"), SIZE[s])

                for s in range(4, 8):
                    load_in(s)
                stream(la, w_in, 8, 6, 8, IN_SLABS)
                load_in(14)
                at = 0
                for j, size in enumerate(MLA_SIZE):
                    load(la, S_MLA + j, w_mla[bass.ds(la, 1), :, at:at + size].rearrange("a p n -> (a p) n"), size)
                    at += size
                stream(la, w_in, S_MLA + len(MLA_SIZE), 24, S_MLA, IN_SLABS)
                stream(la, w_out, S_OUT, 16, 0, 16)
                stream(la, w_gu, S_GU, 4 * GU_CHUNKS, 0, 4 * GU_CHUNKS)
                stream(la, w_dn, S_DN, DN_SLABS, 0, DN_SLABS)
            for c in range(4):
                sp.wait_ge(x_ready, 4 + LAYERS * 8 - 4 + c + 1)
                sp.dma_start(out_d[:, :, c * CH:(c + 1) * CH].rearrange("t p n -> p t n"),
                             x[:, :, c * CH:(c + 1) * CH]).then_inc(stored, 16)
            sp.wait_ge(stored, 64)

        @block.gpsimd
        def _(pool):
            g = nc.gpsimd
            own = [0]
            layer = [0]

            def link(ins):
                own[0] += 1
                ins.then_inc(pool_own, 1)
                pool.wait_ge(pool_own, layer[0] * POOL_OWN + own[0])

            def rstd(out, mean, var, n):
                link(g.tensor_tensor(var, mean, eps_row[:, 0:n], ALU.add))
                return g.tensor_tensor(out, var, mhalf[:, 0:n], ALU.pow)

            for buf, value in ((mhalf[:], -0.5), (eps_row[:], EPS), (inv_head[:], 1.0 / P),
                               (inv_rank[:, 0:2], 1.0 / Q_RANK), (yss[:, :, 4:5], EPS), (inv_rank[:, 2:4], 1.0 / KV_RANK)):
                g.memset(buf, value).then_inc(set_up, 1)
            pool.wait_ge(set_up, 6)

            def set_gain(at):
                g.tensor_copy(g_mix[:], gain_all[:, at, :].rearrange("p a n -> p (a n)")).then_inc(gain_ok, 1)

            pool.wait_ge(s_load, 16)
            set_gain(slice(LAYERS - 1, LAYERS))
            pool.wait_ge(x_load[0], 16)
            pool.sem_inc(x_ready, 1)
            pool.wait_ge(loaded[0], 16)
            for c in range(1, 4):
                g.dma_start(x[:, :, c * CH:(c + 1) * CH],
                            x_d[:, :, c * CH:(c + 1) * CH].rearrange("t p n -> p t n")).then_inc(x_load[c], 16)
            g.dma_start(rope[:], rope_d).then_inc(c_load, 16)
            g.dma_start(axial[:], axial_d).then_inc(c_load, 16)
            g.dma_start(small_all[:, :, 0:N_COLS], small_d).then_inc(c_load, 16)
            g.dma_start(small_all[:, :, G_CQN:N_SMALL],
                        gqa_d.to_broadcast([P, LAYERS, 2 * P])).then_inc(c_load, 16)
            for c in range(1, 4):
                pool.wait_ge(x_load[c], 16)
                pool.sem_inc(x_ready, 1)
            pool.wait_ge(c_load, 64)
            pool.wait_ge(lam_a, 1)
            g.tensor_tensor(lam_d1[:], lam_e[:, :, 0], lam_e[:, :, 1], ALU.subtract).then_inc(set_up, 1)
            pool.wait_ge(set_up, 7)
            g.tensor_tensor(lam_all[:], lam_d1[:], small_all[:, :, LAM0], ALU.add).then_inc(set_up, 1)
            pool.wait_ge(set_up, 8)
            pool.wait_ge(rel_sum, 1)
            rows = rel_rows.rearrange("h (q r) -> h q r", r=REL)
            for n in range(4):
                g.dma_start(rows[2 * n:2 * n + 2],
                            relrow_s[2 * n:2 * n + 2, 0:REL].unsqueeze(1).to_broadcast([2, P, REL])).then_inc(rel_out, 16)
                pool.wait_ge(rel_out, 16 * n + 16)

            with pool.Fori(0, LAYERS) as la:
                layer[0] = la
                own[0] = 0
                pool.wait_ge(x_ready, la * 8 + 4)
                g.tensor_copy(small[:], small_all[:, bass.ds(la, 1), :].rearrange("p a n -> p (a n)")).then_inc(params, 1)
                link(g.tensor_copy(lam[:], lam_all[:, bass.ds(la, 1)]))
                g.tensor_tensor(gsub[:], small[:, G_SUB:G_SUB + 1], small[:, ONE_LAM0:ONE_LAM0 + 1], ALU.mult).then_inc(params, 1)
                pool.wait_ge(xsq, la * 2 + 1)
                rstd(rs[:], xss[:], xvar[:], TT).then_inc(rs_ok, 1)

                def fetch_bias(n):
                    src = bass.AP(rel_rows.tensor, 2 * n * P * REL + P - 1, [[REL - 1, P], [P * REL, 2], [1, SEQ + P]])
                    g.dma_start(bias[:, 2 * n:2 * n + 2, :], src).then_inc(rel_in, 16)

                fetch_bias(0)
                fetch_bias(1)
                lat = qkv[:, :, B_CQ:B_CQ + 768]
                tl = tmp[:].rearrange("p (t n) -> p t n", t=TT)
                pool.wait_ge(acc_free, la * CHUNKS + ORDER["in", 1] + 3)
                g.tensor_tensor(tl, lat, lat, ALU.mult).then_inc(sq_b, 1)
                pool.wait_ge(ss_b, la + 1)
                link(g.tensor_tensor(bmean[:], bss[:], inv_rank[:], ALU.mult))
                rstd(brs[:], bmean[:], bvar[:], 4).then_inc(brs_ok, 1)

                def rotate(x1, x2, cos, sin, t1, t2, t3, t4, done=None):
                    g.tensor_tensor(t1, x1, cos, ALU.mult)
                    g.tensor_tensor(t2, x2, sin, ALU.mult)
                    g.tensor_tensor(t3, x2, cos, ALU.mult)
                    link(g.tensor_tensor(t4, x1, sin, ALU.mult))
                    g.tensor_tensor(x1, t1, t2, ALU.subtract)
                    link(g.tensor_tensor(x2, t3, t4, ALU.add))

                def parts(shape):
                    n = int(np.prod(shape))
                    return [shaped(tmp[:, i * 384:i * 384 + n], shape) for i in range(4)]

                def shaped(ap, shape):
                    if len(shape) == 2:
                        return ap.rearrange("p (a b) -> p a b", a=shape[0])
                    return ap.rearrange("p (a b c) -> p a b c", a=shape[0], b=shape[1])

                kp = qkv[:, :, B_KPE:B_KPE + ROPE]
                rotate(kp[:, :, 0:32], kp[:, :, 32:64], rope[:, :, 0, :], rope[:, :, 1, :], *parts((2, 32)))
                g.sem_inc(kpe_ok, 1)
                fetch_bias(2)
                pool.wait_ge(acc_free, la * CHUNKS + ORDER["mla", 1] + 3)
                for t in range(TT):
                    qh = qb[:, t, :].rearrange("p (h d) -> p h d", d=NOPE + ROPE)[:, :, NOPE:NOPE + ROPE]
                    cos = rope[:, t, 0, :].unsqueeze(1).to_broadcast([P, 4, 32])
                    sin = rope[:, t, 1, :].unsqueeze(1).to_broadcast([P, 4, 32])
                    rotate(qh[:, :, 0:32], qh[:, :, 32:64], cos, sin, *parts((4, 32)))
                g.sem_inc(bq_ok, 1)
                fetch_bias(3)
                cqk = qkv[:, :, C_Q:C_Q + 768]
                pool.wait_ge(acc_free, la * CHUNKS + ORDER["in", 3] + 3)
                link(g.tensor_tensor(tl, cqk, cqk, ALU.mult))
                g.sem_inc(sq_c, 1)
                pool.wait_ge(ss_c, la + 1)
                link(g.tensor_tensor(cmean[:], css[:], inv_head[:], ALU.mult))
                link(rstd(crs[:], cmean[:], cvar[:], 12))
                for t in range(TT):
                    heads = cqk[:, t, :].rearrange("p (h d) -> p h d", d=P)
                    ri = crs[:, t * 6:t * 6 + 6].unsqueeze(2).to_broadcast([P, 6, P])
                    link(g.tensor_tensor(heads, heads, ri, ALU.mult))
                    for h0, nh, col in ((0, C_HEADS, G_CQN), (C_HEADS, C_KV, G_CKN)):
                        gain = small[:, col:col + P].unsqueeze(1).to_broadcast([P, nh, P])
                        link(g.tensor_tensor(heads[:, h0:h0 + nh, :], heads[:, h0:h0 + nh, :], gain, ALU.mult))
                for t in range(TT):
                    pair = cqk[:, t, :].rearrange("p (h f w d) -> p h f w d", f=2, w=2, d=32)
                    cos = axial[:, 0, t].unsqueeze(1).to_broadcast([P, 6, 2, 32])
                    sin = axial[:, 1, t].unsqueeze(1).to_broadcast([P, 6, 2, 32])
                    rotate(pair[:, :, :, 0, :], pair[:, :, :, 1, :], cos, sin, *parts((6, 2, 32)))
                g.sem_inc(c_ok, 1)
                pool.wait_ge(ao_ss, la + 1)
                link(g.tensor_tensor(amean[:], ass[:], inv_head[:, 0:8], ALU.mult))
                rstd(ars[:], amean[:], avar[:], 8).then_inc(ao_rs, 1)
                pool.wait_ge(y_sum, la * 2 + 1)
                g.tensor_tensor(rsy[:], ysum[:], mhalf[:, 0:TT], ALU.pow).then_inc(rsy_ok, 1)
                pool.wait_ge(xsq, la * 2 + 2)
                rstd(rs[:], xss[:], xvar[:], TT).then_inc(rs_ok, 1)
                set_gain(bass.ds(la, 1))
                pool.wait_ge(y_sum, la * 2 + 2)
                g.tensor_tensor(rsy[:], ysum[:], mhalf[:, 0:TT], ALU.pow).then_inc(rsy_ok, 1)
                if own[0] != POOL_OWN:
                    raise ValueError(f"POOL_OWN = {own[0]}")

        @block.scalar
        def _(act):
            a = nc.scalar
            la_ = [0]

            def hi(s, size=SLAB):
                k, par = s
                act.wait_ge(loaded[par], (la_[0] * (SLABS // 2) + k) * 16 + 16)
                act.wait_ge(used, (la_[0] * (SLABS // 2) + k) * 2 + (par + 1))
                a.activation(w_hi[:, par, 0:size], raw[:, par, 0:size], ACT.Copy).then_inc(hi_done, 1)

            def hx(n):
                gain = g_mix if n == 0 else small[:, G_FFN:G_FFN + KT]
                for b in range(8):
                    if n == 0 and b in (1, 2):
                        hi((0, b - 1))
                    act.wait_ge(hx_tr, (la_[0] * 2 + n) * 8 + b + 1)
                    for kk in range(2):
                        k = 2 * b + kk
                        last = a.activation(h_hi[:, k, :], ps[:, 4 + b % 4, kk * SEQ:(kk + 1) * SEQ],
                                            ACT.Copy, scale=gain[:, k:k + 1])
                    last.then_inc(hx_hi, 1)
                hi((1, 0) if n == 0 else (S_GU // 2 + 1, 0))
                act.wait_ge(x_ready, la_[0] * 8 + (4 * n + 4))
                if n == 1:
                    act.dma_start(gpost, post_ffn[bass.ds(la_[0], 1), :].to_broadcast([P, D])).then_inc(post_load, 16)
                for t in range(TT):
                    last = a.activation(y[:, t, :], x[:, t, :], ACT.Square, scale=D ** -0.5,
                                        accum_out=xss[:, t:t + 1])
                last.then_inc(xsq, 1)

            def y_squares(end, banks, quarter, before, between=None):
                act.wait_ge(*end)
                act.wait_ge(y_sq, before * 2)
                for t in range(TT):
                    if t == 1:
                        act.wait_ge(y_g1, before)
                    a.activation(tmp[:, t * CH:(t + 1) * CH], ps[:, banks + t, :], ACT.Square, scale=D ** -0.5,
                                 accum_out=yss[:, t, quarter]).then_inc(y_sq, 1)
                    if t == 0 and between:
                        between()

            def front_hi(s):
                hi((s // 2, s % 2), SIZE[s] if s < S_GU else SLAB)

            def take(chunk):
                la, (kind, c), bank = la_[0], chunk, 2 * (ORDER[chunk] % 2)
                if kind == "out":
                    y_squares((used, la * SLABS + (last_slab(chunk) + 3)), bank, slice(c, c + 1), la * 8 + (c + 1))
                    return
                if chunk == ("in", 0):
                    act.wait_ge(rs_ok, la * 2 + 1)
                if chunk == ("mla", 0):
                    act.wait_ge(brs_ok, la + 1)
                if chunk == ("mla", 2):
                    act.wait_ge(mla_mid, la + 1)
                else:
                    act.wait_ge(used, la * SLABS + (last_slab(chunk) + 3))
                for t in range(TT):
                    if kind == "in":
                        at, n = IN_ORDER[c]
                        dst, scale = qkv[:, t, at:at + n], rs[:, t:t + 1]
                    else:
                        n = (512, 256, 512, 512)[c]
                        at = (0, 512, 0, 512)[c]
                        dst = (qb if c < 2 else kvb)[:, t, at:at + n]
                        scale = brs[:, 2 * (c // 2) + t:2 * (c // 2) + t + 1]
                    last = a.activation(dst, ps[:, bank + t, 0:n], ACT.Copy, scale=scale)
                last.then_inc(acc_free, 1)

            def attend(half, late):
                la = la_[0]
                if not late:
                    if (i := unit(half, 0)) is not None:
                        g, h = UNITS[i]
                        act.wait_ge(t_done, la * NU + (i + 1))
                        last = a.activation(qkT, ps[:, 4, :], ACT.Copy)
                        if g == "B":
                            last = a.activation(qrT[:], ps[0:64, 6, 0:SEQ], ACT.Copy)
                            if h == 0:
                                last = a.activation(kpeT[:], ps[0:64, 6, SEQ:2 * SEQ], ACT.Copy)
                        last.then_inc(t_out, 1)
                    if (i := unit(half, TURN)) is not None:
                        act.wait_ge(pt_done, la * NU + (i + 1))
                        a.activation(PT, ps[:, 6 + 1, :], ACT.Copy).then_inc(pt_out, 1)
                        if i == NU - 1:
                            act.dma_start(gpost, post_mix[bass.ds(la, 1), :].to_broadcast([P, D])).then_inc(post_load, 16)
                    if half == LATENT_AT:
                        act.wait_ge(params, la * 2 + 1)
                        for b in range(3):
                            act.wait_ge(ct_tr, la * 3 + (b + 1))
                            for kk in range(2):
                                k = 2 * b + kk
                                last = a.activation(c_hi[:, k, :], ps[:, 4 + b, kk * SEQ:(kk + 1) * SEQ],
                                                    ACT.Copy, scale=small[:, G_CQ + k:G_CQ + k + 1])
                            last.then_inc(ct_hi, 1)
                    return
                if half == 2 * S_OUT:
                    act.wait_ge(used, la * SLABS + (S_OUT + 2))
                    act.wait_ge(o_out, la * NU + 8)
                    a.activation(h_hi[:, EARLY:8, :].rearrange("p h (t d) -> p h t d", t=TT),
                                 heads_out[:, 2:4], ACT.Copy).then_inc(mix_hi, 1)
                if (i := unit(half, EXP)) is not None:
                    g, h = UNITS[i]
                    act.wait_ge(m_ok, la * NU + (i + 1))
                    for m in range(2 if g == "A" else 1):
                        for t in range(TT):
                            cols = slice(t * SEQ, (t + 1) * SEQ)
                            e = prob[:, i % 2, m, cols]
                            src, scale = (e, 1.0) if g in "AD" else (ps[:, 5, cols], scale_of(g))
                            last = a.activation(e, src, ACT.Exp, bias=nmax[:, i % 2, 2 * m + t:2 * m + t + 1],
                                                scale=scale, accum_out=esum[:, i % 2, 2 * m + t:2 * m + t + 1])
                    last.then_inc(e_done, 1)
                if (i := unit(half, OUT)) is not None:
                    g, h = UNITS[i]
                    act.wait_ge(o_done, la * NU + (i + 1))
                    o = ps[:, 7, 0:SEQ]
                    k = MIX_AT[g] + h
                    if k < EARLY or g == "D":
                        a.activation(heads_hi_lo(k)[0][:, k, :], o, ACT.Copy).then_inc(o_hi, 1)
                    else:
                        dst = qkv[:, :, A_Q + h * P:A_Q + (h + 1) * P] if g == "A" else heads_out[:, h]
                        a.activation(dst, o.rearrange("p (t d) -> p t d", t=TT), ACT.Copy).then_inc(o_out, 1)
                if half in A_TURN:
                    b = A_TURN.index(half)
                    act.wait_ge(params, la * 2 + 2)
                    act.wait_ge(ao_tr, la * 2 + (b + 1))
                    k = MIX_AT["A"] + 2 * b
                    a.activation(h_hi[:, k:k + 2, :].rearrange("p k n -> p (k n)"), ps[:, 4, :],
                                 ACT.Copy, scale=gsub[:]).then_inc(ao_hi, 1)

            act.dma_start(ident[:], ident_d).then_inc(i_load, 16)
            act.dma_start(lam_in[:].rearrange("p l f d -> p (l f d)"),
                          lam_d.to_broadcast([P, LAYERS * 256])).then_inc(l_load, 16)
            act.wait_ge(lam_v, 2)
            a.activation(lam_e[:].rearrange("p l f -> p (l f)"), lam_e[:].rearrange("p l f -> p (l f)"),
                         ACT.Exp).then_inc(lam_a, 1)
            with act.Fori(0, LAYERS) as la:
                la_[0] = la
                act.wait_ge(gain_ok, la + 1)
                hx(0)
                for s in range(S_GU):
                    attend(2 * s, False)
                    if s >= 1:
                        if s >= 2:
                            front_hi(s + 1)
                        if s - 1 in ENDED:
                            take(ENDED[s - 1])
                    attend(2 * s, True)
                    attend(2 * s + 1, False)
                    attend(2 * s + 1, True)
                    if s == last_slab(("mla", 2)):
                        take(("mla", 2))
                take(("out", 3))
                front_hi(S_GU + 1)
                hx(1)
                act.wait_ge(rs_ok, la * 2 + 2)

                def gu_chunk(n, par, turn):
                    k = n * 2 + S_GU // 2
                    if turn:
                        hi((k + 1, 0))
                    hi((k + 1, 1))
                    if turn:
                        turned(n - 1, 1 - par)
                    hi((k + 2, 0))
                    if isinstance(n, int) and n == GU_CHUNKS - 1:
                        act.wait_ge(ht_out, la * GU_CHUNKS + (2 + 2))
                        hid_hi(0, 0)
                        hid_hi(1, 1)
                    at_end = isinstance(n, int) and n == GU_CHUNKS - 1
                    if not at_end:
                        hi((k + 2, 1))
                    act.wait_ge(used, la * SLABS + n * 4 + (S_GU + 6))
                    for t in range(TT):
                        last = a.activation(sg[:, par, t, :], ps[:, 2 * par + t, 0:256], ACT.Silu,
                                            scale=rs[:, t:t + 1])
                    last.then_inc(sw_g, 1)
                    if at_end:
                        hi((k + 2, 1))

                def turned(n, par):
                    act.wait_ge(ht_tr, la * GU_CHUNKS + n + 1)
                    dst = big[:, bass.ds(n * 512, 512)]
                    a.activation(dst, ps[:, 4 + par, :], ACT.Copy).then_inc(ht_out, 1)

                def hid_hi(j, par):
                    src = big[:, bass.ds(j * 512, 512)]
                    a.activation(c_hi[:, 2 * par:2 * par + 2, :].rearrange("p k n -> p (k n)"), src,
                                 ACT.Copy).then_inc(hid_hi_ok, 1)

                gu_chunk(0, 0, False)
                with act.Fori(0, 10) as i:
                    gu_chunk(i * 2 + 1, 1, True)
                    gu_chunk(i * 2 + 2, 0, True)
                gu_chunk(21, 1, True)
                turned(21, 1)
                def dn(k, par):
                    act.wait_ge(used, (la * (SLABS // 2) + (S_DN // 2) + k) * 2 + (par + 1))

                act.wait_ge(ht_out, la * GU_CHUNKS + (GU_CHUNKS + 2))
                for half in range(2):
                    with act.Fori(0, 10) as i:
                        for par in range(2):
                            dn(i + (1 + 11 * half), par)
                            hid_hi(i * 2 + (2 + par), par)
                            hi((i + (S_DN // 2 + 1 + 11 * half), par))
                    def second_half(par):
                        dn(11, par)
                        hid_hi(par, par)
                        hi((S_DN // 2 + 11, par))

                    if half == 0:
                        second_half(0)
                    for q in range(2):
                        y_squares((dn_first, la * 2 + (half + 1)) if q == 0 else (used, la * SLABS + (S_DN + 22 * half + 24)),
                                  4 * half + 2 * q, slice(2 * half + q, 2 * half + q + 1), la * 8 + (5 + 2 * half + q),
                                  (lambda: second_half(1)) if half == 0 and q == 1 else None)

        @block.tensor
        def _(pe):
            t_ = nc.tensor
            la_ = [0]

            def split_product(out, k, t, w, wl, first, last, hh=h_hi, hl=h_lo):
                cols = slice(t * P, (t + 1) * P)
                t_.matmul(out, hh[:, k, cols], w, start=first, stop=False)
                t_.matmul(out, hh[:, k, cols], wl, start=False, stop=False)
                return t_.matmul(out, hl[:, k, cols], w, start=False, stop=last)

            def slab_ready(k, par):
                pe.wait_ge(lo_done, (la_[0] * (SLABS // 2) + k) * 2 + (par + 3))

            def chunk(k, c, par, middle=None, first=False):
                pe.wait_ge(acc_free, c + 1)
                for j in range(4):
                    slab_ready(k + j // 2, j % 2)
                    for kk in range(4):
                        kt = 4 * j + kk
                        if first and j == 0 and kk >= 1:
                            hx(1, kk)
                        if first and kk % 2 == 0:
                            pe.wait_ge(hx_lo, la_[0] * 16 + (8 + 2 * j + kk // 2 + 1))
                        for t in range(TT):
                            last = split_product(ps[:, 2 * par + t, :], kt, t,
                                                 slab_view(w_hi, j % 2, 4, CH)[:, kk, :],
                                                 slab_view(w_lo, j % 2, 4, CH)[:, kk, :],
                                                 kt == 0, kt == KT - 1)
                    last.then_inc(used, 1)
                    if j == 1 and middle:
                        middle()

            def turn(out, src):
                return t_.transpose(out, src, ident[:])

            def hx(n, pair):
                pe.wait_ge(x_ready, la_[0] * 8 + (4 * n + pair + 1))
                for b in (2 * pair, 2 * pair + 1):
                    if b >= 4:
                        pe.wait_ge(hx_lo, (la_[0] * 2 + n) * 8 + b - 3)
                    for kk in range(2):
                        for t in range(TT):
                            k = 2 * b + kk
                            last = turn(ps[:, 4 + b % 4, kk * SEQ + t * P:kk * SEQ + (t + 1) * P],
                                        x[:, t, k * P:(k + 1) * P])
                    last.then_inc(hx_tr, 1)

            pe.wait_ge(r_load, 16)
            t_.matmul(ps[0:8, 0, :], rel_s, oh_s, start=True, stop=True).then_inc(rel_mm, 1)
            pe.wait_ge(rel_sum, 1)
            pe.wait_ge(i_load, 16)

            with pe.Fori(0, LAYERS) as la:
                la_[0] = la
                hx(0, 0)

                def transposes(i):
                    g, h = UNITS[i]
                    if i >= 1:
                        pe.wait_ge(t_out, la * NU + i)
                    if g == "D" and h >= 2:
                        pe.wait_ge(ao_lo, la * 2 + (h - 1))
                    if h == 0:
                        ready = {"B": ("mla", 3), "C": ("in", 3), "A": ("in", 5), "D": ("in", 8)}[g]
                        pe.wait_ge(acc_free, la * CHUNKS + (ORDER[ready] + 3))
                    if g == "C" and h == 0:
                        pe.wait_ge(c_ok, la + 1)
                    if g == "B" and h == 0:
                        pe.wait_ge(bq_ok, la + 1)
                        pe.wait_ge(kpe_ok, la + 1)
                    for t in range(TT):
                        q, k, _ = qkv_of(g, h, t)
                        turn(ps[:, 4, t * P:(t + 1) * P], q)
                        last = turn(ps[:, 4, SEQ + t * P:SEQ + (t + 1) * P], k)
                        if g == "B":
                            at = h * (NOPE + ROPE) + NOPE
                            last = turn(ps[0:64, 6, t * P:(t + 1) * P], qb[:, t, at:at + ROPE])
                            if h == 0:
                                last = turn(ps[0:64, 6, SEQ + t * P:SEQ + (t + 1) * P],
                                            qkv[:, t, B_KPE:B_KPE + ROPE])
                    last.then_inc(t_done, 1)

                def scores(i):
                    g, h = UNITS[i]
                    pe.wait_ge(t_out, la * NU + i + 1)
                    for m in range(2 if g == "A" else 1):
                        rows = slice(64 * m, 64 * m + 64) if g == "A" else slice(0, P)
                        for t in range(TT):
                            out = ps[:, 5 + m, t * SEQ:(t + 1) * SEQ]
                            last = t_.matmul(out, qkT[rows, t * P:(t + 1) * P], qkT[rows, SEQ:2 * SEQ],
                                             start=True, stop=g != "B")
                            if g == "B":
                                last = t_.matmul(out, qrT[:, t * P:(t + 1) * P], kpeT[:], start=False, stop=True)
                    last.then_inc(s_done, 1)

                def prob_transposes(i):
                    pe.wait_ge(p_ok, la * NU + i + 1)
                    if i >= 1:
                        pe.wait_ge(o_out, la * NU + i)
                    for kt in range(TT):
                        for t in range(TT):
                            last = turn(ps[:, 7, kt * SEQ + t * P:kt * SEQ + (t + 1) * P],
                                        prob[:, i % 2, 0, t * SEQ + kt * P:t * SEQ + (kt + 1) * P])
                    last.then_inc(pt_done, 1)

                def outputs(i):
                    g, h = UNITS[i]
                    pe.wait_ge(pt_out, la * NU + i + 1)
                    if g in "AD" and h == 0:
                        pe.wait_ge(acc_free, la * CHUNKS + (ORDER["in", 6 if g == "A" else 9] + 3))
                    pt = PT.rearrange("p (k n) -> p k n", k=TT)
                    if g == "A":
                        for t in range(TT):
                            for kt in range(TT):
                                last = t_.matmul(ps[:, 7, t * P:(t + 1) * P], pt[:, kt, t * P:(t + 1) * P],
                                                 qkv_of(g, h, kt)[2], start=kt == 0, stop=kt == TT - 1)
                    else:
                        for kt in range(TT):
                            last = t_.matmul(ps[:, 7, 0:SEQ], qkv_of(g, h, kt)[2], pt[:, kt, :],
                                             start=kt == 0, stop=kt == TT - 1)
                    last.then_inc(o_done, 1)

                def steps(half):
                    for step, do in ((TURN, prob_transposes), (SCORE, scores), (0, transposes), (OUT, outputs)):
                        if (i := unit(half, step)) is not None:
                            do(i)
                    if half in A_TURN:
                        b = A_TURN.index(half)
                        pe.wait_ge(ao_n, la + 1)
                        i = max(START[f] for f in START if f <= half)
                        pe.wait_ge(t_out, la * NU + (i + 1))
                        if b == 1:
                            pe.wait_ge(ao_lo, la * 2 + 1)
                        for kk in range(2):
                            for t in range(TT):
                                last = turn(ps[:, 4, kk * SEQ + t * P:kk * SEQ + (t + 1) * P],
                                            qkv[:, t, A_Q + (2 * b + kk) * P:A_Q + (2 * b + kk + 1) * P])
                        last.then_inc(ao_tr, 1)
                    if half == LATENT_AT:
                        pe.wait_ge(acc_free, la * CHUNKS + (ORDER["in", 1] + 3))
                        for b in range(3):
                            for kk in range(2):
                                for t in range(TT):
                                    k = 2 * b + kk
                                    last = turn(ps[:, 4 + b, kk * SEQ + t * P:kk * SEQ + (t + 1) * P],
                                                qkv[:, t, B_CQ + k * P:B_CQ + (k + 1) * P])
                            last.then_inc(ct_tr, 1)

                for s, pieces in enumerate(FRONT):
                    steps(2 * s)
                    tiles = [(f, kk) for f in pieces for kk in range(f[3])]
                    slab_ready(s // 2, s % 2)
                    at = 0
                    for place, ((kind, c, k0, kts, n), kk) in enumerate(tiles):
                        order, k = ORDER[kind, c], k0 + kk
                        begins, ends = (kk == 0, kk == kts - 1) if kind == "mla" else (k == 0, k == KT - 1)
                        if begins:
                            pe.wait_ge(acc_free, la * CHUNKS + (order + 1))
                        if place == len(tiles) // 2:
                            steps(2 * s + 1)
                        if s == 0 and kk >= 1:
                            hx(0, kk)
                        if (kind, c) == ("in", 0) and kk % 2 == 0:
                            pe.wait_ge(hx_lo, la * 16 + (k // 2 + 1))
                        if (kind, c, kk) == ("mla", 0, 0):
                            pe.wait_ge(ct_lo, la * 3 + 3)
                        if kind == "out" and c < 2:
                            if k == 0:
                                pe.wait_ge(o_out, la * NU + EARLY)
                            if k == EARLY:
                                pe.wait_ge(mix_lo, la + 1)
                            if k == MIX_AT["A"]:
                                pe.wait_ge(ao_lo, la * 2 + 2)
                            if k == MIX_AT["D"]:
                                pe.wait_ge(o_out, la * NU + NU)
                        hh, hl = {"mla": (c_hi, c_lo), "out": heads_hi_lo(k), "in": (h_hi, h_lo)}[kind]
                        for t in range(TT):
                            last = split_product(ps[:, 2 * (order % 2) + t, 0:n], k, t,
                                                 w_hi[:, s % 2, at:at + n], w_lo[:, s % 2, at:at + n],
                                                 begins, ends, hh, hl)
                        at += n
                        if (kind, c) == ("mla", 2) and ends:
                            last.then_inc(mla_mid, 1)
                    last.then_inc(used, 1)
                hx(1, 0)

                def hid_turn(n, par):
                    pe.wait_ge(acc_free, la * CHUNKS + n + (C_GU + 3))
                    pe.wait_ge(ht_out, la * GU_CHUNKS + n + 1)
                    for kk in range(2):
                        for t in range(TT):
                            last = turn(ps[:, 4 + par, kk * SEQ + t * P:kk * SEQ + (t + 1) * P],
                                        act_tile[:, par, t, kk * P:(kk + 1) * P])
                    last.then_inc(ht_tr, 1)

                def gu_chunk(n, par, turned):
                    middle = (lambda: hid_turn(n - 1, 1 - par)) if turned else None
                    chunk(n * 2 + S_GU // 2, la * CHUNKS + n + C_GU, par, middle, first=isinstance(n, int) and n == 0)

                gu_chunk(0, 0, False)
                with pe.Fori(0, 10) as i:
                    gu_chunk(i * 2 + 1, 1, True)
                    gu_chunk(i * 2 + 2, 0, True)
                gu_chunk(21, 1, True)

                def dn_quarter(par, half, q, first, last):
                    for kk in range(2):
                        for t in range(TT):
                            w = slab_view(w_hi, par, 2, 1024)[:, kk, q * CH:(q + 1) * CH]
                            wl = slab_view(w_lo, par, 2, 1024)[:, kk, q * CH:(q + 1) * CH]
                            mm = split_product(ps[:, 4 * half + 2 * q + t, :], 2 * par + kk, t, w, wl,
                                               first and kk == 0, last and kk == 1, c_hi, c_lo)
                    return mm

                def dn_slab(k, par, half, first, last):
                    slab_ready(k, par)
                    pe.wait_ge(hid_lo_ok, la * DN_SLABS + (k - S_DN // 2) * 2 + (par + 1))
                    for q in range(2):
                        if first and half == 0:
                            pe.wait_ge(acc_free, la * CHUNKS + (C_DN + 1 + q))
                        mm = dn_quarter(par, half, q, first, last)
                        if last and q == 0:
                            mm.then_inc(dn_first, 1)
                    mm.then_inc(used, 1)

                for half in range(2):
                    k = S_DN // 2 + 11 * half
                    if half == 1:
                        pe.wait_ge(ht_out, la * GU_CHUNKS + (GU_CHUNKS + 2))
                    dn_slab(k, 0, half, True, False)
                    if half == 0:
                        hid_turn(21, 1)
                    dn_slab(k, 1, half, False, False)
                    with pe.Fori(0, 9) as i:
                        for par in range(2):
                            dn_slab(i + (k + 1), par, half, False, False)
                    dn_slab(k + 10, 0, half, False, False)
                    dn_slab(k + 10, 1, half, False, True)

        @block.vector
        def _(dve):
            v = nc.vector
            la_ = [0]
            own = [0]

            def link(ins):
                own[0] += 1
                ins.then_inc(dve_own, 1)
                dve.wait_ge(dve_own, la_[0] * DVE_OWN + own[0])

            def lo(s, size=SLAB):
                k, par = s
                dve.wait_ge(hi_done, (la_[0] * (SLABS // 2) + k) * 2 + (par + 1))
                v.tensor_tensor(w_lo[:, par, 0:size], raw[:, par, 0:size], w_hi[:, par, 0:size].bitcast(F32),
                                ALU.subtract).then_inc(lo_done, 1)

            def hx_b(n, b):
                gain = g_mix if n == 0 else small[:, G_FFN:G_FFN + KT]
                dve.wait_ge(hx_hi, (la_[0] * 2 + n) * 8 + (b + 1))
                for kk in range(2):
                    k = 2 * b + kk
                    last = v.scalar_tensor_tensor(h_lo[:, k, :], ps[:, 4 + b % 4, kk * SEQ:(kk + 1) * SEQ],
                                                  gain[:, k:k + 1], h_hi[:, k, :].bitcast(F32),
                                                  ALU.mult, ALU.subtract)
                last.then_inc(hx_lo, 1)

            def y_gain(end, sq, bank, cols, n, between=None):
                dve.wait_ge(post_load, la_[0] * 32 + (16 + 16 * n))
                dve.wait_ge(*end)
                v.tensor_tensor(y[:, 1, cols], ps[:, bank + 1, :], gpost[:, cols], ALU.mult).then_inc(y_g1, 1)
                dve.wait_ge(y_sq, sq * 2 - 1)
                v.tensor_tensor(y[:, 0, cols], ps[:, bank, :], gpost[:, cols], ALU.mult).then_inc(y_g0, 1)
                if between:
                    between()
                dve.wait_ge(y_g0, sq - 1)
                dve.wait_ge(y_sq, sq * 2)
                dve.sem_inc(acc_free, 1)

            def x_update(n):
                v.tensor_reduce(ysum[:], yss[:], AX_X, ALU.add).then_inc(y_sum, 1)
                dve.wait_ge(rsy_ok, la_[0] * 2 + n + 1)
                dve.wait_ge(acc_free, la_[0] * CHUNKS + (C_GU + 2 if n == 0 else CHUNKS + 2))
                if n == 1:
                    for c in range(4):
                        quarter(c)
                    return
                quarter(0)
                hx_b(1, 0)
                hx_b(1, 1)
                quarter(1)
                front_lo(S_GU + 1)
                quarter(2)
                hx_b(1, 2)
                hx_b(1, 3)
                quarter(3)
                for b in range(4, 8):
                    hx_b(1, b)

            def quarter(c):
                cols = slice(c * CH, (c + 1) * CH)
                for t in range(TT):
                    last = v.scalar_tensor_tensor(x[:, t, cols], y[:, t, cols], rsy[:, t:t + 1], x[:, t, cols],
                                                  ALU.mult, ALU.add)
                last.then_inc(x_ready, 1)

            def front_lo(s):
                lo((s // 2, s % 2), SIZE[s] if s < S_GU else SLAB)

            dve.sem_inc(lo_done, 2)
            dve.sem_inc(used, 2)
            dve.sem_inc(acc_free, 2)
            dve.sem_inc(ht_out, 2)
            dve.sem_inc(y_sq, 2)
            dve.wait_ge(l_load, 16)
            for la in range(LAYERS):
                for f in range(2):
                    last = v.tensor_tensor(lam_prod[:, 2 * la + f, :], lam_in[:, la, 2 * f, :],
                                           lam_in[:, la, 2 * f + 1, :], ALU.mult)
            last.then_inc(lam_v, 1)
            dve.wait_ge(lam_v, 1)
            v.tensor_reduce(lam_e[:].rearrange("p l f -> p (l f)"), lam_prod[:], AX_X, ALU.add).then_inc(lam_v, 1)
            dve.wait_ge(rel_mm, 1)
            v.tensor_tensor(relrow_s, ps[0:8, 0, :], lnc_s, ALU.add).then_inc(rel_sum, 1)

            with dve.Fori(0, LAYERS) as la:
                la_[0] = la
                own[0] = 0
                dve.wait_ge(gain_ok, la + 1)
                for b in range(8):
                    hx_b(0, b)
                    if b == 0:
                        lo((0, 0))
                    if b == 3:
                        lo((0, 1))
                def softmax_max(i):
                    g, h = UNITS[i]
                    b = i % 2
                    dve.wait_ge(s_done, la * NU + i + 1)
                    if g in "AD":
                        if g == "A" and h == 0:
                            dve.wait_ge(rel_in, la * 64 + 64)
                        maps = 2 if g == "A" else 1
                        for m in range(maps):
                            for t in range(TT):
                                cols = slice(t * SEQ, (t + 1) * SEQ)
                                at = (1 - t) * P
                                last = v.scalar_tensor_tensor(prob[:, b, m, cols], ps[:, 5 + m, cols], scale_of(g),
                                                              bias[:, (0 if g == "A" else 4) + h, at:at + SEQ],
                                                              ALU.mult, ALU.add)
                        link(last)
                        v.tensor_reduce(nmax[:, b, 0:2 * maps],
                                        prob[:, b, 0:maps, :].rearrange("p m (t n) -> p (m t) n", t=TT),
                                        AX_X, ALU.max, negate=True).then_inc(m_ok, 1)
                    else:
                        link(v.tensor_reduce(mx[:, b, 0:2], ps[:, 5, :].rearrange("p (t n) -> p t n", t=TT),
                                             AX_X, ALU.max))
                        v.tensor_scalar(nmax[:, b, 0:2], mx[:, b, 0:2], -scale_of(g), None, ALU.mult).then_inc(m_ok, 1)

                def softmax_norm(i):
                    g, h = UNITS[i]
                    b = i % 2
                    dve.wait_ge(e_done, la * NU + i + 1)
                    if g == "A":
                        if h == 0:
                            dve.wait_ge(params, la * 2 + 2)
                        link(v.reciprocal(rsum[:, b, :], esum[:, b, :]))
                        link(v.tensor_scalar(rlam[:, b, :], rsum[:, b, 2:4], lam[:], None, ALU.mult))
                        for t in range(TT):
                            cols = slice(t * SEQ, (t + 1) * SEQ)
                            last = v.tensor_scalar(prob[:, b, 1, cols], prob[:, b, 1, cols], rlam[:, b, t:t + 1],
                                                   None, ALU.mult)
                        link(last)
                    else:
                        link(v.reciprocal(rsum[:, b, 0:2], esum[:, b, 0:2]))
                    for t in range(TT):
                        cols = slice(t * SEQ, (t + 1) * SEQ)
                        if g == "A":
                            last = v.scalar_tensor_tensor(prob[:, b, 0, cols], prob[:, b, 0, cols],
                                                          rsum[:, b, t:t + 1], prob[:, b, 1, cols],
                                                          ALU.mult, ALU.subtract)
                        else:
                            last = v.tensor_scalar(prob[:, b, 0, cols], prob[:, b, 0, cols], rsum[:, b, t:t + 1],
                                                   None, ALU.mult)
                    last.then_inc(p_ok, 1)

                def attend(half, late):
                    if not late:
                        if (i := unit(half, SCORE)) is not None:
                            softmax_max(i)
                        return
                    if half == 2 * S_OUT:
                        dve.wait_ge(mix_hi, la + 1)
                        for k in range(EARLY, 8):
                            last = v.tensor_tensor(h_lo[:, k, :].rearrange("p (t d) -> p t d", t=TT),
                                                   heads_out[:, k - 4],
                                                   h_hi[:, k, :].bitcast(F32).rearrange("p (t d) -> p t d", t=TT),
                                                   ALU.subtract)
                        last.then_inc(mix_lo, 1)
                    if (i := unit(half, EXP)) is not None:
                        softmax_norm(i)
                    i = unit(half, OUT)
                    k = MIX_AT[UNITS[i][0]] + UNITS[i][1] if i is not None else -1
                    if 0 <= k < EARLY or k >= MIX_AT["D"]:
                        n = k if k < EARLY else EARLY + k - MIX_AT["D"]
                        hh, hl = heads_hi_lo(k)
                        dve.wait_ge(o_hi, la * (EARLY + 4) + (n + 1))
                        v.tensor_tensor(hl[:, k, :], ps[:, 7, 0:SEQ], hh[:, k, :].bitcast(F32),
                                        ALU.subtract).then_inc(o_out, 1)
                    if half == LATENT_AT:
                        dve.wait_ge(params, la * 2 + 1)
                        for b in range(3):
                            dve.wait_ge(ct_hi, la * 3 + (b + 1))
                            for kk in range(2):
                                k = 2 * b + kk
                                last = v.scalar_tensor_tensor(c_lo[:, k, :], ps[:, 4 + b, kk * SEQ:(kk + 1) * SEQ],
                                                              small[:, G_CQ + k:G_CQ + k + 1],
                                                              c_hi[:, k, :].bitcast(F32), ALU.mult, ALU.subtract)
                            last.then_inc(ct_lo, 1)
                    tl = tmp[:].rearrange("p (t n) -> p t n", t=TT)
                    if half == LATENT_AT + 2:
                        dve.wait_ge(sq_b, la + 1)
                        v.tensor_reduce(bss[:, 0:2], tl[:, :, 0:Q_RANK], AX_X, ALU.add)
                        v.tensor_reduce(bss[:, 2:4], tl[:, :, Q_RANK:768], AX_X, ALU.add).then_inc(ss_b, 1)
                    if half == SQ_C_AT:
                        dve.wait_ge(sq_c, la + 1)
                        v.tensor_reduce(css[:], tmp[:].rearrange("p (g d) -> p g d", d=P), AX_X,
                                        ALU.add).then_inc(ss_c, 1)
                    if half == A_SQUARE:
                        dve.wait_ge(o_out, la * NU + 12)
                        link(v.tensor_tensor(qkv[:, :, A_K:A_K + 512], qkv[:, :, A_Q:A_Q + 512],
                                             qkv[:, :, A_Q:A_Q + 512], ALU.mult))
                        for t in range(TT):
                            last = v.tensor_reduce(ass[:, 4 * t:4 * t + 4],
                                                   qkv[:, t, A_K:A_K + 512].rearrange("p (h d) -> p h d", d=P),
                                                   AX_X, ALU.add)
                        last.then_inc(ao_ss, 1)
                    if half == A_NORM:
                        dve.wait_ge(ao_rs, la + 1)
                        for t in range(TT):
                            o = qkv[:, t, A_Q:A_Q + 512].rearrange("p (h d) -> p h d", d=P)
                            last = v.tensor_tensor(o, o, ars[:, 4 * t:4 * t + 4].unsqueeze(2).to_broadcast([P, 4, P]),
                                                   ALU.mult)
                        last.then_inc(ao_n, 1)
                    if half in A_TURN:
                        n = A_TURN.index(half)
                        k = MIX_AT["A"] + 2 * n
                        dve.wait_ge(ao_hi, la * 2 + (n + 1))
                        v.scalar_tensor_tensor(h_lo[:, k:k + 2, :].rearrange("p k n -> p (k n)"), ps[:, 4, :], gsub[:],
                                               h_hi[:, k:k + 2, :].rearrange("p k n -> p (k n)").bitcast(F32),
                                               ALU.mult, ALU.subtract).then_inc(ao_lo, 1)

                def out_gain(c):
                    y_gain((used, la * SLABS + (last_slab(("out", c)) + 3)), la * 8 + (c + 2), 2 * (ORDER["out", c] % 2), slice(c * CH, (c + 1) * CH), 0)

                for s in range(S_GU):
                    attend(2 * s, False)
                    if s >= 1:
                        front_lo(s + 1)
                        if ENDED.get(s - 1, ("", 0))[0] == "out":
                            out_gain(ENDED[s - 1][1])
                    attend(2 * s, True)
                    attend(2 * s + 1, False)
                    attend(2 * s + 1, True)
                out_gain(3)
                x_update(0)

                def hid_lo(j, par, count):
                    dve.wait_ge(hid_hi_ok, count)
                    src = big[:, bass.ds(j * 512, 512)]
                    hh = c_hi[:, 2 * par:2 * par + 2, :].rearrange("p k n -> p (k n)").bitcast(F32)
                    v.tensor_tensor(c_lo[:, 2 * par:2 * par + 2, :].rearrange("p k n -> p (k n)"), src, hh,
                                    ALU.subtract).then_inc(hid_lo_ok, 1)

                base = la * 44

                def gu_chunk(n, par, at_end=False):
                    k = n * 2 + S_GU // 2
                    lo((k + 1, 0))
                    lo((k + 1, 1))
                    lo((k + 2, 0))
                    if at_end:
                        hid_lo(0, 0, base + 1)
                        hid_lo(1, 1, base + 2)
                    else:
                        lo((k + 2, 1))
                    dve.wait_ge(sw_g, la * GU_CHUNKS + n + 1)
                    for t in range(TT):
                        last = v.scalar_tensor_tensor(act_tile[:, par, t, :], ps[:, 2 * par + t, 256:512],
                                                      rs[:, t:t + 1], sg[:, par, t, :], ALU.mult, ALU.mult)
                    last.then_inc(acc_free, 1)
                    if at_end:
                        lo((k + 2, 1))

                with dve.Fori(0, GU_CHUNKS // 2 - 1) as i:
                    gu_chunk(i * 2, 0)
                    gu_chunk(i * 2 + 1, 1)
                gu_chunk(GU_CHUNKS - 2, 0)
                gu_chunk(GU_CHUNKS - 1, 1, True)

                for half in range(2):
                    with dve.Fori(0, 10) as i:
                        for par in range(2):
                            hid_lo(i * 2 + (2 + par), par, base + i * 2 + (22 * half + 3 + par))
                            lo((i + (S_DN // 2 + 1 + 11 * half), par))
                    def second_half(par):
                        hid_lo(par, par, base + 22 + par + 1)
                        lo((S_DN // 2 + 11, par))

                    if half == 0:
                        second_half(0)
                    for q in range(2):
                        y_gain((dn_first, la * 2 + (half + 1)) if q == 0 else (used, la * SLABS + (S_DN + 22 * half + 24)),
                               la * 8 + (4 + 2 * half + q + 2), 4 * half + 2 * q,
                               slice((2 * half + q) * CH, (2 * half + q + 1) * CH), 1,
                               (lambda: second_half(1)) if half == 0 and q == 1 else None)
                x_update(1)
                if own[0] != DVE_OWN:
                    raise ValueError(f"DVE_OWN = {own[0]}")


def constants():
    rel = np.arange(511) - 255
    n = np.abs(rel)
    nf = np.maximum(n, 8).astype(np.float32)
    large = 8 + (np.log(nf / np.float32(8)) / np.float32(np.log(1024 / 8)) * np.float32(8)).astype(np.int32)
    bucket = np.where(rel > 0, 16, 0) + np.where(n < 8, n, np.minimum(large, 15))
    onehot = np.zeros((32, 512), np.float32)
    onehot[bucket, np.arange(511)] = 1.0
    count = np.zeros(511)
    for w, r in ((128, 1), (512, 4), (2048, 16)):
        count += (n <= w // 2) & (n % r == 0)
    lncount = np.zeros((32, 512), np.float32)
    lncount[4:8, :511] = np.where(count > 0, np.log(np.maximum(count, 1)), -1e30)
    pos = np.arange(SEQ)

    def angles(p, dim):
        inv = (np.float32(10000.0) ** (-np.arange(0, dim, 2, dtype=np.float32) / np.float32(dim))).astype(np.float32)
        ang = (p.astype(np.float32)[:, None] * inv[None, :]).astype(np.float32).astype(np.float64)
        return np.stack([np.cos(ang), np.sin(ang)]).astype(np.float32)

    rope = angles(pos, 64).reshape(2, TT, P, 32).transpose(2, 1, 0, 3)
    ax = np.stack([angles(pos // 64, 64), angles(pos % 64, 64)], 1)
    axial = ax.reshape(2, 2, TT, P, 32).transpose(3, 0, 2, 1, 4)
    return {"onehot_d": onehot, "lncount_d": lncount, "ident_d": np.eye(P, dtype=np.float32),
            "rope_d": np.ascontiguousarray(rope), "axial_d": np.ascontiguousarray(axial)}


def lay_out(v):
    L = LAYERS
    asc = np.ascontiguousarray
    w = v["w_in"]
    pad = np.zeros((L, D, PAD), np.float32)
    w = np.concatenate([w[:, :, :PAD_AT], pad, w[:, :, PAD_AT:]], 2)
    slabs = lambda m, c: m.reshape(L, 4, 4, P, c, CH).transpose(0, 4, 1, 3, 2, 5).reshape(L, c, 4, P, SLAB)
    w_in = slabs(w, 10)[:, [at // CH for at, _ in IN_ORDER]]
    narrow = w_in[:, 1].reshape(L, 4, P, 4, CH)[..., :CH - PAD].transpose(0, 2, 1, 3, 4).reshape(L, P, KT, CH - PAD)
    packed = np.zeros((L, 3, P, SLAB), np.float32)
    for j, pieces in enumerate(FRONT[4:7]):
        k0, n = pieces[0][2:4]
        packed[:, j, :, :SIZE[4 + j]] = narrow[:, :, k0:k0 + n].reshape(L, P, -1)
    w_in = np.concatenate([w_in[:, 0], packed, w_in[:, 2:].reshape(L, 32, P, SLAB)], 1).reshape(L * IN_SLABS, P, SLAB)
    w_out = v["w_out"].reshape(L, 4, 512, D)[:, [1, 2, 0, 3]].reshape(L, D, D)
    w_out = slabs(w_out, 4).reshape(L, 16, P, SLAB)
    w_out = w_out[:, [4 * c + k0 // 4 for (kind, c, k0, *_), in FRONT[S_OUT:]]].reshape(L * 16, P, SLAB)
    gu = v["w_gate_up"].reshape(L, 4, 4, P, 2, GU_CHUNKS, 256).transpose(0, 5, 1, 3, 2, 4, 6)
    dn = v["w_down"].reshape(L, 22, 2, P, 2, 1024).transpose(0, 4, 1, 3, 2, 5)
    uq = v["mla_w_uq"].reshape(L, 4, P, 768).transpose(0, 2, 1, 3)
    ukv = v["mla_w_ukv"].reshape(L, 2, P, 1024).transpose(0, 2, 1, 3)
    mla = np.concatenate([m.reshape(L, P, -1) for m in (uq[..., :512], uq[..., 512:], ukv[..., :512], ukv[..., 512:])], 2)
    col = lambda m: m.reshape(L, -1, P).transpose(2, 0, 1)
    lam0 = [0.8 - 0.6 * np.exp(-0.3 * n) for n in range(L)]
    const = np.broadcast_to(np.array([[a, 1.0 - a] for a in lam0], np.float32), (P, L, 2))
    small = np.concatenate([col(v[n]) for n in ("norm_ffn_pre", "mla_q_norm", "mla_kv_norm", "diff_subln")]
                           + [const], 2)
    arrays = {
        "x_d": v["x"].reshape(TT, P, D), "w_in": w_in, "w_mla": mla,
        "w_out": w_out, "w_gu": gu.reshape(L * GU_CHUNKS * 4, P, SLAB),
        "w_dn": dn.reshape(L * DN_SLABS, P, SLAB), "small_d": small,
        "gain_d": col(v["norm_mix_pre"])[:, [(n + 1) % L for n in range(L)]],
        "gqa_d": np.concatenate([v["gqa_q_norm"], v["gqa_k_norm"]], 1)[None],
        "post_mix": v["norm_mix_post"], "post_ffn": v["norm_ffn_post"],
        "lam_d": v["diff_lambda"].reshape(1, -1), }
    arrays.update(constants())
    arrays["rel_d"] = np.concatenate([arrays.pop("onehot_d"), v["rel_bias"], arrays.pop("lncount_d")], 1)
    return {n: asc(m) for n, m in arrays.items()}


def kernel(**inputs):
    import concourse.bacc as bacc
    from concourse.bass_utils import run_bass_kernel_spmd

    nc = bacc.Bacc("TRN2", target_bir_lowering=False, num_devices=1)
    arrays = lay_out({n: np.asarray(m) for n, m in inputs.items()})
    args = {n: nc.dram_tensor(n, m.shape, mybir.dt.from_np(m.dtype), kind="ExternalInput").ap()
            for n, m in arrays.items()}
    out = nc.dram_tensor("out_d", (TT, P, D), F32, kind="ExternalOutput").ap()
    build(nc, out_d=out, **args)
    r = run_bass_kernel_spmd(nc, [arrays], core_ids=[0])
    return r.results[0]["out_d"].reshape(1, SEQ, D)
```
